# Optimizing a Trainium2 kernel written in Bass

```python
import jax, jax.numpy as jnp
from jax import lax
import numpy as np

D_MODEL = 1024
BATCH = 1
SEQ = 1024
DEPTH = 2

N_A_LAYERS = DEPTH // 2
N_B_LAYERS = DEPTH - N_A_LAYERS

HG_HEADS = 8
HG_DK = 128
HG_DV = D_MODEL // HG_HEADS
HG_KEY_WIDTH = HG_HEADS * HG_DK
HG_VAL_WIDTH = HG_HEADS * HG_DV
HG_CHUNK = 64

SWA_Q_HEADS = 16
SWA_KV_HEADS = 4
SWA_GROUP = SWA_Q_HEADS // SWA_KV_HEADS
SWA_HEAD_DIM = 64
SWA_WIDTH = SWA_Q_HEADS * SWA_HEAD_DIM
SWA_KV_WIDTH = SWA_KV_HEADS * SWA_HEAD_DIM
WINDOW = 128
SWA_BLOCK = WINDOW

MEM_TOKENS = 256
MEM_HEADS = 4
MEM_HEAD_DIM = 128
MEM_WIDTH = MEM_HEADS * MEM_HEAD_DIM

ROPE_THETA = 10000.0
NORM_EPS = 1e-6

A_IN_SPLITS = (HG_KEY_WIDTH, HG_KEY_WIDTH, HG_VAL_WIDTH, HG_VAL_WIDTH, MEM_WIDTH, MEM_WIDTH)
B_IN_SPLITS = (SWA_WIDTH, SWA_WIDTH, MEM_WIDTH, MEM_WIDTH)
A_IN_WIDTH = sum(A_IN_SPLITS)
B_IN_WIDTH = sum(B_IN_SPLITS)
A_OUT_WIDTH = HG_VAL_WIDTH + MEM_WIDTH
B_OUT_WIDTH = SWA_WIDTH + MEM_WIDTH

kernel_name = "yoco_hgrn2_swa_sink_memory_trunk"

def rms_norm(x, g):
    xf = x.astype(jnp.float32)
    y = xf * lax.rsqrt(jnp.mean(xf * xf, axis=-1, keepdims=True) + NORM_EPS)
    return (y * g.astype(jnp.float32)).astype(x.dtype)

def split_cols(z, sizes):
    return jnp.split(z, list(np.cumsum(sizes)[:-1]), axis=-1)

def rope_tables(positions, dim):
    inv_freq = ROPE_THETA ** (-jnp.arange(0, dim, 2, dtype=jnp.float32) / dim)
    ang = positions.astype(jnp.float32)[..., None] * inv_freq
    return jnp.cos(ang), jnp.sin(ang)

def apply_rope(x, cos, sin):
    xf = x.astype(jnp.float32)
    x1, x2 = jnp.split(xf, 2, axis=-1)
    c = cos[:, :, None, :]
    s = sin[:, :, None, :]
    return jnp.concatenate([x1 * c - x2 * s, x2 * c + x1 * s], axis=-1).astype(x.dtype)

def memory_attention(mq, mem_n, w_mem_kv):
    b, s, _ = mq.shape
    q = mq.reshape(b, s, MEM_HEADS, MEM_HEAD_DIM)
    kv = jnp.einsum('bmd,de->bme', mem_n, w_mem_kv)
    k, v = jnp.split(kv, 2, axis=-1)
    k = k.reshape(b, -1, MEM_HEADS, MEM_HEAD_DIM)
    v = v.reshape(b, -1, MEM_HEADS, MEM_HEAD_DIM)
    scores = jnp.einsum('bshd,bmhd->bhsm', q, k).astype(jnp.float32) * (MEM_HEAD_DIM ** -0.5)
    p = jax.nn.softmax(scores, axis=-1)
    o = jnp.einsum('bhsm,bmhd->bshd', p.astype(v.dtype), v)
    return o.reshape(b, s, MEM_WIDTH)

def hgrn2_mixer(q_pre, f_pre, i_in, lb, out_norm_g):
    b, s, _ = q_pre.shape
    n_chunks = s // HG_CHUNK
    lbf = lb.astype(jnp.float32).reshape(HG_HEADS, HG_DK)
    fp = f_pre.astype(jnp.float32).reshape(b, s, HG_HEADS, HG_DK)
    log_f = jnp.logaddexp(jnp.log(lbf), jnp.log1p(-lbf) + jax.nn.log_sigmoid(fp))
    k = (1.0 - lbf) * jax.nn.sigmoid(-fp)
    q = jax.nn.silu(q_pre.astype(jnp.float32)).reshape(b, s, HG_HEADS, HG_DK)
    v = i_in.astype(jnp.float32).reshape(b, s, HG_HEADS, HG_DV)

    def to_chunks(t):
        return t.reshape(b, n_chunks, HG_CHUNK, HG_HEADS, -1).transpose(1, 0, 3, 2, 4)

    causal = jnp.tril(jnp.ones((HG_CHUNK, HG_CHUNK), dtype=bool))

    def step(state, xs):
        qc, kc, vc, lfc = xs
        cum = jnp.cumsum(lfc, axis=2)
        inter = jnp.einsum('bhtk,bhkv->bhtv', qc * jnp.exp(cum), state)
        diff = cum[:, :, :, None, :] - cum[:, :, None, :, :]
        decay = jnp.exp(jnp.where(causal[:, :, None], diff, -jnp.inf))
        scores = jnp.einsum('bhtsk,bhsk->bhts', qc[:, :, :, None, :] * decay, kc)
        intra = jnp.einsum('bhts,bhsv->bhtv', scores, vc)
        last = cum[:, :, -1, :]
        k_dec = kc * jnp.exp(last[:, :, None, :] - cum)
        state = jnp.exp(last)[..., None] * state + jnp.einsum('bhsk,bhsv->bhkv', k_dec, vc)
        return state, inter + intra

    state0 = jnp.zeros((b, HG_HEADS, HG_DK, HG_DV), jnp.float32)
    _, o = lax.scan(step, state0, (to_chunks(q), to_chunks(k), to_chunks(v), to_chunks(log_f)))
    o = o.transpose(1, 0, 3, 2, 4).reshape(b, s, HG_HEADS, HG_DV)
    o = o * lax.rsqrt(jnp.mean(o * o, axis=-1, keepdims=True) + NORM_EPS)
    o = o * out_norm_g.astype(jnp.float32).reshape(HG_HEADS, HG_DV)
    return o.reshape(b, s, HG_VAL_WIDTH).astype(q_pre.dtype)

def sliding_window_sink_attention(q, k, v, sinks):
    b, s = q.shape[:2]
    nb = s // SWA_BLOCK
    qb = q.reshape(b, nb, SWA_BLOCK, SWA_KV_HEADS, SWA_GROUP, SWA_HEAD_DIM)
    kb = k.reshape(b, nb, SWA_BLOCK, SWA_KV_HEADS, SWA_HEAD_DIM)
    vb = v.reshape(b, nb, SWA_BLOCK, SWA_KV_HEADS, SWA_HEAD_DIM)
    pad_k = jnp.zeros_like(kb[:, :1])
    pad_v = jnp.zeros_like(vb[:, :1])
    k2 = jnp.concatenate([jnp.concatenate([pad_k, kb[:, :-1]], axis=1), kb], axis=2)
    v2 = jnp.concatenate([jnp.concatenate([pad_v, vb[:, :-1]], axis=1), vb], axis=2)
    scores = jnp.einsum('bnqhgd,bnkhd->bnhgqk', qb, k2).astype(jnp.float32) * (SWA_HEAD_DIM ** -0.5)
    blk = jnp.arange(nb)[:, None, None]
    qpos = blk * SWA_BLOCK + jnp.arange(SWA_BLOCK)[None, :, None]
    kpos = (blk - 1) * SWA_BLOCK + jnp.arange(2 * SWA_BLOCK)[None, None, :]
    dist = qpos - kpos
    mask = (dist >= 0) & (dist < WINDOW) & (kpos >= 0)
    scores = jnp.where(mask[None, :, None, None], scores, -jnp.inf)
    sink = sinks.astype(jnp.float32).reshape(SWA_KV_HEADS, SWA_GROUP)[None, None, :, :, None, None]
    m = jnp.maximum(jnp.max(scores, axis=-1, keepdims=True), sink)
    p = jnp.exp(scores - m)
    p = p / (jnp.sum(p, axis=-1, keepdims=True) + jnp.exp(sink - m))
    o = jnp.einsum('bnhgqk,bnkhd->bnqhgd', p.astype(v2.dtype), v2)
    return o.reshape(b, s, SWA_WIDTH)

def shared_kv(h, kv_norm_g, w_kv_shared, cos, sin):
    b, s, _ = h.shape
    kv = jnp.einsum('bsd,de->bse', rms_norm(h, kv_norm_g), w_kv_shared)
    k, v = jnp.split(kv, 2, axis=-1)
    k = apply_rope(k.reshape(b, s, SWA_KV_HEADS, SWA_HEAD_DIM), cos, sin)
    v = v.reshape(b, s, SWA_KV_HEADS, SWA_HEAD_DIM)
    return k, v

def setup_inputs(seed: int = 0) -> dict:
    key = jax.random.key(seed)
    ks = jax.random.split(key, 20)

    def nrm(k, shape, scale):
        return jax.random.normal(k, shape, jnp.float32) * scale

    x = nrm(ks[0], (BATCH, SEQ, D_MODEL), 1.0)
    mem = nrm(ks[1], (BATCH, MEM_TOKENS, D_MODEL), 1.0)
    offsets = jax.random.randint(ks[2], (BATCH, 1), 0, 4096, dtype=jnp.int32)
    positions = offsets + jnp.arange(SEQ, dtype=jnp.int32)[None, :]
    return {
        "x": x,
        "mem": mem,
        "positions": positions,
        "pre_norm_g": 1.0 + nrm(ks[3], (DEPTH, D_MODEL), 0.02),
        "post_norm_g": 1.0 + nrm(ks[4], (DEPTH, D_MODEL), 0.02),
        "mem_norm_g": 1.0 + nrm(ks[5], (DEPTH, D_MODEL), 0.02),
        "w_mem_kv": nrm(ks[6], (DEPTH, D_MODEL, 2 * MEM_WIDTH), D_MODEL ** -0.5),
        "a_w_in": nrm(ks[7], (N_A_LAYERS, D_MODEL, A_IN_WIDTH), D_MODEL ** -0.5),
        "a_lb_logits": nrm(ks[8], (N_A_LAYERS + 1, HG_KEY_WIDTH), 0.5),
        "a_out_norm_g": 1.0 + nrm(ks[9], (N_A_LAYERS, HG_VAL_WIDTH), 0.02),
        "a_w_out": nrm(ks[10], (N_A_LAYERS, A_OUT_WIDTH, D_MODEL), A_OUT_WIDTH ** -0.5),
        "kv_norm_g": 1.0 + nrm(ks[11], (D_MODEL,), 0.02),
        "w_kv_shared": nrm(ks[12], (D_MODEL, 2 * SWA_KV_WIDTH), D_MODEL ** -0.5),
        "b_w_in": nrm(ks[13], (N_B_LAYERS, D_MODEL, B_IN_WIDTH), D_MODEL ** -0.5),
        "b_sinks": nrm(ks[14], (N_B_LAYERS, SWA_Q_HEADS), 0.5),
        "b_w_out": nrm(ks[15], (N_B_LAYERS, B_OUT_WIDTH, D_MODEL), B_OUT_WIDTH ** -0.5),
    }

def reference(x, mem, positions, pre_norm_g, post_norm_g, mem_norm_g, w_mem_kv,
              a_w_in, a_lb_logits, a_out_norm_g, a_w_out,
              kv_norm_g, w_kv_shared, b_w_in, b_sinks, b_w_out):
    b, s, _ = x.shape
    cos, sin = rope_tables(positions, SWA_HEAD_DIM)
    lb_all = jnp.cumsum(jax.nn.softmax(a_lb_logits.astype(jnp.float32), axis=0), axis=0)
    h = x
    k_sh = None
    v_sh = None
    for layer in range(DEPTH):
        xn = rms_norm(h, pre_norm_g[layer])
        mem_n = rms_norm(mem, mem_norm_g[layer])
        if layer < N_A_LAYERS:
            z = jnp.einsum('bsd,de->bse', xn, a_w_in[layer])
            q_pre, f_pre, i_in, g_main, mq, g_mem = split_cols(z, A_IN_SPLITS)
            o_main = hgrn2_mixer(q_pre, f_pre, i_in, lb_all[layer], a_out_norm_g[layer])
            o_main = o_main * jax.nn.silu(g_main)
            o_mem = memory_attention(mq, mem_n, w_mem_kv[layer]) * jax.nn.silu(g_mem)
            y = jnp.einsum('bse,ed->bsd', jnp.concatenate([o_main, o_mem], axis=-1), a_w_out[layer])
        else:
            if layer == N_A_LAYERS:
                k_sh, v_sh = shared_kv(h, kv_norm_g, w_kv_shared, cos, sin)
            j = layer - N_A_LAYERS
            z = jnp.einsum('bsd,de->bse', xn, b_w_in[j])
            q, g_main, mq, g_mem = split_cols(z, B_IN_SPLITS)
            q = apply_rope(q.reshape(b, s, SWA_Q_HEADS, SWA_HEAD_DIM), cos, sin)
            o_main = sliding_window_sink_attention(q, k_sh, v_sh, b_sinks[j]) * jax.nn.silu(g_main)
            o_mem = memory_attention(mq, mem_n, w_mem_kv[layer]) * jax.nn.silu(g_mem)
            y = jnp.einsum('bse,ed->bsd', jnp.concatenate([o_main, o_mem], axis=-1), b_w_out[j])
        h = h + rms_norm(y, post_norm_g[layer])
    return h


_drawn_inputs = setup_inputs


def setup_inputs(seed=0):
    import zlib

    import numpy as np

    out = dict(_drawn_inputs(seed))
    spreads = {}
    factors = {'mem_norm_g': 7.435, 'a_out_norm_g': 10.677, 'kv_norm_g': 17.197, 'b_sinks': 48.527}
    for name, (base, spread) in spreads.items():
        noise = np.random.default_rng([zlib.crc32(name.encode()), seed]).standard_normal(out[name].shape)
        drawn = base * np.exp(spread * noise) if base else spread * noise
        out[name] = __import__('jax').numpy.asarray(drawn.astype(out[name].dtype))
    for name, factor in factors.items():
        out[name] = (out[name] * factor).astype(out[name].dtype)
    return out
```

```python
from contextlib import ExitStack

import numpy as np

import concourse.bass as bass
from concourse import mybir

F32 = mybir.dt.float32
F32R = mybir.dt.float32r
I32 = mybir.dt.int32
U8 = mybir.dt.uint8
ACT = mybir.ActivationFunctionType
ALU = mybir.AluOpType
AX = mybir.AxisListType

P = 128
D = 1024
T = 1024
KB = D // P
HALF = 512
HEADS = 8
CH = T // P
LEVELS = 7
MT = 256
MH = 4
EB = 12
GROUPS = 4
DH = 64
EPS = 1e-6
BIG = float(2.0 ** 62)
MEM_SCALE = float(P) ** -0.5
SWA_SCALE = float(DH) ** -0.5
NEG = -1e38
PI = float(np.pi)

N_H = 0
N_AM = N_H + 4 * HEADS
N_AO = N_AM + 4 * MH
N_K = N_AO + KB
N_S = N_K + 4
N_BM = N_S + 4 * GROUPS
N_BO = N_BM + 4 * MH

SWA_ROUNDS = (4, 7, 10, 13, 16, 19, 22, 25, 28, 30)


class Tile:

    def __init__(self, base, stage, i):
        self.slot = i % 2
        self.n = base + 4 * stage + i
        self.before = base // 2 + 2 * stage + i // 2


def wait(eng, semaphore, value):
    if not (isinstance(value, int) and value <= 0):
        eng.wait_ge(semaphore, value)


def build(nc, x, mem, positions, pre_g, post_g, mem_g, w_mem, a_w_in, lb_logits, out_g, a_w_out, kv_g,
          w_kv, b_w_in, sinks, b_w_out, c_ident, c_level, c_window, c_freq, h_dram, k_dram, out):
    ctx = ExitStack()
    with ctx:
        def sem(name):
            return ctx.enter_context(nc.semaphore(name))

        def psum(name, shape, dt=F32):
            return ctx.enter_context(nc.psum_tensor(name, shape, dt))

        place = [-(-nc.sbuf_base // 64) * 64]

        def sb(name, shape, dt=F32, at=None):
            size = int(np.prod(shape[1:])) * (1 if dt == U8 else 4)
            if at is None:
                at = place[0]
                place[0] += -(-size // 64) * 64
            return nc.alloc_sbuf_tensor_at(name, shape, dt, offset=at)

        X = sb("X", [P, 16, T], F32R)
        O = sb("O", [P, EB, T])
        w_raw = sb("w_raw", [P, 2, EB, P])
        w_hi = sb("w_hi", [P, 2, EB, P], F32R)
        w_lo = sb("w_lo", [P, 2, EB, P], F32R)
        ident = sb("ident", [P, P])
        ones = sb("ones", [P, P])
        level_mask = sb("level_mask", [P, LEVELS, HALF], U8)
        window = sb("window", [P, 2 * P])
        pre_col = sb("pre_col", [P, 2, KB])
        post_col = sb("post_col", [P, 2, KB])
        mem_col = sb("mem_col", [P, 2, KB])
        kv_col = sb("kv_col", [P, KB])
        out_col = sb("out_col", [P, HEADS])
        lb2 = sb("lb2", [P, 2, HEADS])
        lb = sb("lb", [P, HEADS])
        oml = sb("oml", [P, HEADS])
        lbt = sb("lbt", [P, 2, HEADS])
        freq = sb("freq", [P, 1])
        sink_b = sb("sink_b", [P, 4 * GROUPS])
        eps_c = sb("eps_c", [P, 1])
        ST = sb("ST", [P, 2, P])
        EL = sb("EL", [P, CH])
        pad = sb("pad", [P, 1])
        sm_max = sb("sm_max", [P, 2, 4])
        sm_neg = sb("sm_neg", [P, 2, 4])
        sm_den = sb("sm_den", [P, 2, 4])
        sm_inv = sb("sm_inv", [P, 2, 4])
        sm_snk = sb("sm_snk", [P, 2, 4])

        arena = place[0]
        ROW = 4 * T

        def ar(name, row, shape, dt=F32):
            return sb(name, shape, dt, at=arena + int(row * ROW))

        CUM = ar("CUM", 0, [P, T])
        KK = ar("KK", 1, [P, T])
        Q = ar("Q", 2, [P, 2, T])
        E2 = ar("E2", 4, [P, 2, T])
        KH = ar("KH", 6, [P, 2, T])
        QH = ar("QH", 8, [P, 2, HALF])
        PT = ar("PT", 9, [P, T])
        TV = ar("TV", 10, [P, T])
        SQ = ar("SQ", 11, [P, HALF])
        RN = ar("RN", 11.5, [P, HALF])
        XS = E2
        RB0 = PT
        MHI = ar("MHI", 0, [P, KB, MT], F32R)
        MLO = ar("MLO", 2, [P, KB, MT], F32R)
        MP = ar("MP", 4, [P, 2, 2, MT])
        PTM = ar("PTM", 5, [P, 2, T])
        MS = ar("MS", 5, [P, KB, MT])
        MSQ = ar("MSQ", 7, [P, 2, MT])
        MQ = ar("MQ", 7, [P, T])
        MT1 = ar("MT1", 8, [P, T])
        MX = ar("MX", 8, [P, 2, 2 * MT])
        KM = ar("KM", 9, [P, MT])
        TVM = ar("TVM", 9.25, [P, MT])
        VM = ar("VM", 9.5, [P, 2, P])
        RBM = ar("RBM", 9.75, [P, MT])
        ROPE_AT = 10
        rope_c = ar("rope_c", ROPE_AT, [P, T])
        rope_s = ar("rope_s", ROPE_AT + 1, [P, T])
        assert arena + (ROPE_AT + 2) * ROW <= nc.sbuf_usable_end, (arena, nc.sbuf_usable_end)
        OLO = ar("OLO", 0, [P, 8, T], F32R)
        HR = ar("HR", 0, [P, 2, T])
        XN = ar("XN", 2, [P, 2, T])
        RB = ar("RB", 8, [P, T])
        KST = ar("KST", 0, [P, 2, T])
        KP = ar("KP", 2, [P, 2, T])
        VALL = ar("VALL", 4, [P, CH, 2 * P])
        VG = ar("VG", 6, [P, CH, DH])
        QR = ar("QR", 6.5, [P, 2, T])
        PTS = ar("PTS", 8.5, [P, 2, 4, P])
        LMF = O[:, 8:12, :].rearrange("p a t -> p (a t)")[:, 0:LEVELS * HALF].rearrange("p (l t) -> p l t", l=LEVELS)
        T1 = O[:, 8, :]
        T2 = O[:, 9, :]
        VN = O[:, 10, :]
        KDT = O[:, 11, :]
        RA = O[:, 9, :]
        RTA = ar("RTA", 4, [P, T])
        RTB = ar("RTB", 5, [P, T])
        RTC = ar("RTC", 6, [P, T])
        RTP = ar("RTP", 7, [P, T], I32)
        SM = O[:, 10:12, :]

        Z = psum("Z", [P, 2, T])
        SC = psum("SC", [P, 2, HALF])
        OB = psum("OB", [P, HALF])
        MB = psum("MB", [P, HALF])

        SCF = SC[:, :, :].rearrange("p a t -> p (a t)")

        s_const = sem("s_const")
        s_x_in = [sem(f"s_x_in{e}") for e in range(KB)]
        s_memset = sem("s_memset")
        s_w_in = [sem("s_w_in0"), sem("s_w_in1")]
        s_w_scaled = sem("s_w_scaled")
        s_whi = sem("s_whi")
        s_wlo = sem("s_wlo")
        s_whi_x = sem("s_whi_x")
        s_wlo_x = sem("s_wlo_x")
        s_mm = sem("s_mm")
        s_lb = sem("s_lb")
        s_level = sem("s_level")
        s_lbd = sem("s_lbd")
        s_xsq = sem("s_xsq")
        s_xss = sem("s_xss")
        s_rb0 = sem("s_rb0")
        s_xs = sem("s_xs")
        s_xhi = sem("s_xhi")
        s_xlo = sem("s_xlo")
        s_h_out = [sem("s_h_out0"), sem("s_h_out1")]
        s_sg = sem("s_sg")
        s_clamp = sem("s_clamp")
        s_silu = sem("s_silu")
        s_k = sem("s_k")
        s_cum = sem("s_cum")
        s_tv = sem("s_tv")
        s_vT = sem("s_vT")
        s_vn = sem("s_vn")
        s_dif = sem("s_dif")
        s_dec = sem("s_dec")
        s_hat = sem("s_hat")
        s_qc = sem("s_qc")
        s_kd = sem("s_kd")
        s_el = sem("s_el")
        s_diag = sem("s_diag")
        s_diag_ev = sem("s_diag_ev")
        s_lev = sem("s_lev")
        s_pred = sem("s_pred")
        s_kdT = sem("s_kdT")
        s_kdt = sem("s_kdt")
        s_stm = sem("s_stm")
        s_st = sem("s_st")
        s_fin = sem("s_fin")
        s_osq = sem("s_osq")
        s_og = sem("s_og")
        s_oss = sem("s_oss")
        s_rnl = sem("s_rnl")
        s_rn = sem("s_rn")
        s_on = sem("s_on")
        s_mem_in = sem("s_mem_in")
        s_msq = sem("s_msq")
        s_mss = sem("s_mss")
        s_rbm = sem("s_rbm")
        s_mx = sem("s_mx")
        s_mhi = sem("s_mhi")
        s_mlo = sem("s_mlo")
        s_msg = sem("s_msg")
        s_mclamp = sem("s_mclamp")
        s_mgate = sem("s_mgate")
        s_mq = sem("s_mq")
        s_km = sem("s_km")
        s_tvm = sem("s_tvm")
        s_vmT = sem("s_vmT")
        s_vm = sem("s_vm")
        s_msc = sem("s_msc")
        s_mmax = sem("s_mmax")
        s_mneg = sem("s_mneg")
        s_mexp = sem("s_mexp")
        s_minv = sem("s_minv")
        s_mpn = sem("s_mpn")
        s_mpT = sem("s_mpT")
        s_mpt = sem("s_mpt")
        s_mpv = sem("s_mpv")
        s_mo = sem("s_mo")
        s_pos = sem("s_pos")
        s_rt = sem("s_rt")
        s_rtg = sem("s_rtg")
        s_rope = sem("s_rope")
        s_ohi = sem("s_ohi")
        s_olo = sem("s_olo")
        s_ysq = sem("s_ysq")
        s_y = sem("s_y")
        s_acc = sem("s_acc")
        s_yss = sem("s_yss")
        s_rbl = sem("s_rbl")
        s_rb = sem("s_rb")
        s_hr = [sem("s_hr0"), sem("s_hr1")]
        s_yn = sem("s_yn")
        s_h = sem("s_h")
        s_hsq = sem("s_hsq")
        s_hss = sem("s_hss")
        s_rb2l = sem("s_rb2l")
        s_rb2 = sem("s_rb2")
        s_hn = sem("s_hn")
        s_out = [sem("s_out0"), sem("s_out1")]
        s_ra = sem("s_ra")
        s_rot = sem("s_rot")
        s_k_out = sem("s_k_out")
        s_tvs = sem("s_tvs")
        s_vsT = sem("s_vsT")
        s_vs = sem("s_vs")
        s_kp = sem("s_kp")
        s_kz = sem("s_kz")
        s_vg = sem("s_vg")
        s_ssg = sem("s_ssg")
        s_sclamp = sem("s_sclamp")
        s_sgate = sem("s_sgate")
        s_sc = sem("s_sc")
        s_msk = sem("s_msk")
        s_smax = sem("s_smax")
        s_sm = sem("s_sm")
        s_sneg = sem("s_sneg")
        s_sexp = sem("s_sexp")
        s_sden = sem("s_sden")
        s_sinv = sem("s_sinv")
        s_spn = sem("s_spn")
        s_spT = sem("s_spT")
        s_spt = sem("s_spt")
        s_spv = sem("s_spv")
        s_so = sem("s_so")

        def bc(ap, n):
            return ap.unsqueeze(1).to_broadcast([P, n, ap.shape[-1]])

        block = ctx.enter_context(nc.Block())
        N_CONST = 12

        @block.sync
        def _(sp):
            for dst, src in (
                (ident[:, :], c_ident), (LMF, c_level), (window[:, :], c_window), (freq[:, :], c_freq),
                (pre_col[:, :, :], pre_g), (post_col[:, :, :], post_g), (mem_col[:, :, :], mem_g), (kv_col[:, :], kv_g),
                (out_col[:, :], out_g), (lb2[:, :, :], lb_logits),
                (sink_b[:, :], sinks[0:1, :].to_broadcast([P, 4 * GROUPS])),
            ):
                sp.dma_start(dst, src).then_inc(s_const, 16)
            for e in range(KB):
                sp.dma_start(O[:, e, :], x[:, e, :]).then_inc(s_x_in[e], 16)

            def load(t, src, rows=KB):
                wait(sp, s_wlo, t.n - 1)
                sp.dma_start(w_raw[:, t.slot, 0:rows, :], src).then_inc(s_w_in[t.slot], 16)

            def part(w, at):
                return w[bass.ds(at, 1)].rearrange("a p k c -> (a p) k c")

            def load_head(h):
                for i, which in enumerate((0, 3, 1, 2)):
                    load(Tile(N_H, h, i), part(a_w_in, which * KB + h))

            load_head(0)
            with sp.Fori(1, HEADS) as h:
                load_head(h)

            def load_mem(base, layer, m):
                w, at = (a_w_in, 4 * KB) if layer == 0 else (b_w_in, 2 * KB)
                load(Tile(base, m, 0), part(w, at + MH + m))
                load(Tile(base, m, 1), part(w, at + m))
                load(Tile(base, m, 2), part(w_mem, layer * 2 * MH + m))
                load(Tile(base, m, 3), part(w_mem, layer * 2 * MH + MH + m))

            def load_out(base, layer):
                with sp.Fori(0, KB // 4) as s:
                    for i in range(4):
                        if i == 2:
                            sp.wait_ge(s_wlo_x, layer + 1)
                        load(Tile(base, s, i), part(a_w_out if layer == 0 else b_w_out, 4 * s + i), EB)

            with sp.Fori(0, MH) as m:
                load_mem(N_AM, 0, m)
            load_out(N_AO, 0)
            for i in range(4):
                load(Tile(N_K, 0, i), part(w_kv, i))
            with sp.Fori(0, GROUPS) as g:
                for i in range(4):
                    at = g * 2 + i % 2
                    load(Tile(N_S, g, i), part(b_w_in, at + KB if i < 2 else at))
            with sp.Fori(0, MH) as m:
                load_mem(N_BM, 1, m)
            load_out(N_BO, 1)

        @block.tensor
        def _(pe):
            def x_hi(e, half):
                return X[:, e, half * HALF:(half + 1) * HALF]

            def x_lo(e, half):
                return X[:, 8 + e, half * HALF:(half + 1) * HALF]

            def o_lo(e, half):
                row = X[:, 12 + e, :] if e < 4 else OLO[:, e - 4, :]
                return row[:, half * HALF:(half + 1) * HALF]

            def tile(t, between=None, rows=KB, hi=x_hi, lo=x_lo, ready=None):
                wait(pe, s_wlo, t.n + 1)
                for e in range(rows):
                    if ready:
                        ready(e)
                    wh, wl = w_hi[:, t.slot, e, :], w_lo[:, t.slot, e, :]
                    for a, (w, act) in enumerate(((wh, hi), (wh, lo), (wl, hi))):
                        for half in range(2):
                            mm = nc.tensor.matmul(Z[:, t.slot, half * HALF:(half + 1) * HALF], w, act(e, half),
                                                  start=(e == 0 and a == 0), stop=(e == rows - 1 and a == 2))
                    if e == rows - 1:
                        mm.then_inc(s_mm, 1)
                    for u in (between or {}).get(e, ()):
                        u()

            def mem_tile(t, between=()):
                wait(pe, s_wlo, t.n + 1)
                for e in range(KB):
                    for a, (w, act) in enumerate(((w_hi, MHI), (w_hi, MLO), (w_lo, MHI))):
                        mm = nc.tensor.matmul(Z[:, t.slot, 0:MT], w[:, t.slot, e, :], act[:, e, :],
                                              start=(e == 0 and a == 0), stop=(e == KB - 1 and a == 2))
                mm.then_inc(s_mm, 1)
                for u in between:
                    u()

            pe.wait_ge(s_memset, 1)
            for e in range(KB):
                pe.wait_ge(s_xsq, e + 1)
                for half in range(2):
                    mm = nc.tensor.matmul(SC[:, half, :], ones[:, :], KH[:, e % 2, half * HALF:(half + 1) * HALF],
                                          start=(e == 0), stop=(e == KB - 1))
                mm.then_inc(s_xss, 1)
            pe.wait_ge(s_const, 16 * (N_CONST - 1))

            def hgrn_units(r):
                def v_turn(part):
                    def unit():
                        if part == 0:
                            pe.wait_ge(s_tv, r + 1)
                        else:
                            pe.wait_ge(s_vn, 2 * r + 1)
                        for c in range(4):
                            at = (4 * part + c) * P
                            mm = nc.tensor.transpose(MB[:, c * P:(c + 1) * P], TV[:, at:at + P], ident[:, :])
                        mm.then_inc(s_vT, 1)
                    return unit

                def diagonal(part):
                    def unit():
                        pe.wait_ge(s_k, r + 1)
                        pe.wait_ge(s_silu, 2 * r + 1)
                        if part == 1:
                            pe.wait_ge(s_rnl, 2 * r + 1)
                        for c in range(4):
                            at = (4 * part + c) * P
                            mm = nc.tensor.matmul(SC[:, part, c * P:(c + 1) * P], KK[:, at:at + P],
                                                  q_of(r)[:, at:at + P], start=True, stop=True)
                        mm.then_inc(s_diag, 1)
                    return unit

                def level(l):
                    def unit():
                        pe.wait_ge(s_hat, LEVELS * r + l + 1)
                        if l < 2:
                            pe.wait_ge(s_diag_ev, 2 * r + l + 1)
                        else:
                            pe.wait_ge(s_pred, LEVELS * r + l - 1)
                        for c in range(CH):
                            mm = nc.tensor.matmul(SC[:, l % 2, c * 64:(c + 1) * 64], KH[:, l % 2, c * P:(c + 1) * P],
                                                  QH[:, l % 2, c * 64:(c + 1) * 64], start=True, stop=True)
                        mm.then_inc(s_lev, 1)
                    return unit

                def kd_turn(part):
                    def unit():
                        if part == 0:
                            pe.wait_ge(s_kd, r + 1)
                            pe.wait_ge(s_vn, 2 * r + 2)
                        else:
                            pe.wait_ge(s_kdt, 2 * r + 1)
                        for c in range(4):
                            at = (4 * part + c) * P
                            mm = nc.tensor.transpose(MB[:, c * P:(c + 1) * P], E2[:, 0, at:at + P], ident[:, :])
                        mm.then_inc(s_kdT, 1)
                    return unit

                def chunk(c):
                    def unit():
                        o = OB[:, (c % 4) * P:(c % 4 + 1) * P]
                        if c == 0:
                            pe.wait_ge(s_pred, LEVELS * (r + 1))
                            pe.wait_ge(s_kdt, 2 * r + 2)
                            pe.wait_ge(s_qc, r + 1)
                        if c == 4:
                            pe.wait_ge(s_osq, 2 * r + 1)
                            pe.wait_ge(s_og, 2 * r + 1)
                        mm = nc.tensor.matmul(o, VN[:, c * P:(c + 1) * P], PT[:, c * P:(c + 1) * P],
                                              start=True, stop=(c == 0))
                        if c > 0:
                            pe.wait_ge(s_st, (CH - 1) * r + c)
                            mm = nc.tensor.matmul(o, ST[:, c % 2, :], q_of(r)[:, c * P:(c + 1) * P],
                                                  start=False, stop=True)
                        if c % 4 == 3:
                            mm.then_inc(s_fin, 1)
                        if c < CH - 1:
                            nc.tensor.matmul(MB[:, 0:P], KDT[:, c * P:(c + 1) * P], VN[:, c * P:(c + 1) * P],
                                             start=True, stop=True).then_inc(s_stm, 1)
                    return unit

                def norm(part):
                    def unit():
                        pe.wait_ge(s_osq, 2 * r + part + 1)
                        nc.tensor.matmul(SC[:, part, :], ones[:, :], SQ[:, :], start=True, stop=True).then_inc(s_oss, 1)
                    return unit

                v, d, l, kd, c, n = v_turn, diagonal, level, kd_turn, chunk, norm
                return (
                    {0: [d(0)], 1: [d(1)], 3: [v(0)], 4: [l(0)], 5: [v(1)], 6: [l(1)], 7: [l(2)]},
                    {1: [l(3)], 3: [l(4)], 5: [l(5)], 7: [l(6)]},
                    {0: [kd(0)], 1: [kd(1)], 2: [c(0)], 3: [c(1)], 4: [c(2)], 5: [c(3)], 7: [c(4), n(0)]},
                    {1: [c(5)], 3: [c(6)], 4: [c(7)], 7: [n(1)]},
                )

            def q_of(r):
                return Q[:, r % 2, :] if isinstance(r, int) else Q[:, bass.ds(r % 2, 1), :].rearrange("p a t -> p (a t)")

            def head_stage(h, units):
                tq, tg, tf, tv = (Tile(N_H, h, i) for i in range(4))
                first = isinstance(h, int) and h == 0
                if not first:
                    pe.wait_ge(s_sg, 10 * h - 3)
                tile(tq, units[0], ready=(lambda e: pe.wait_ge(s_xlo, e + 1)) if first else None)
                if not first:
                    pe.wait_ge(s_tv, h)
                tile(tg, units[1])
                pe.wait_ge(s_silu, 2 * h + 1)
                tile(tf, units[2])
                pe.wait_ge(s_silu, 2 * h + 2)
                tile(tv, units[3])

            def alone(steps):
                for step in steps:
                    for e in sorted(step):
                        for u in step[e]:
                            u()

            head_stage(0, (None,) * 4)
            with pe.Fori(1, HEADS) as h:
                head_stage(h, hgrn_units(h - 1))
            alone(hgrn_units(HEADS - 1))

            def mem_prepare(layer):
                for e in range(KB):
                    pe.wait_ge(s_msq, KB * layer + e + 1)
                    nc.tensor.matmul(MB[:, 0:MT], ones[:, :], MSQ[:, e % 2, :], start=(e == 0), stop=(e == KB - 1))\
                      .then_inc(s_mss, 1)

            def mem_units(layer, m):
                r = MH * layer + m

                def v_turn():
                    pe.wait_ge(s_tvm, r + 1)
                    for a in range(2):
                        mm = nc.tensor.transpose(MB[:, a * P:(a + 1) * P], TVM[:, a * P:(a + 1) * P], ident[:, :])
                    mm.then_inc(s_vmT, 1)

                def scores(j):
                    def unit():
                        if j == 0:
                            pe.wait_ge(s_km, r + 1)
                            pe.wait_ge(s_mq, r + 1)
                        if j >= 2:
                            pe.wait_ge(s_mexp, 4 * r + j - 1)
                        for a in range(2):
                            at = (2 * j + a) * P
                            mm = nc.tensor.matmul(SC[:, j % 2, a * MT:(a + 1) * MT], MQ[:, at:at + P], KM[:, :],
                                                  start=True, stop=True)
                        mm.then_inc(s_msc, 1)
                    return unit

                def turn(j):
                    def unit():
                        pe.wait_ge(s_mpn, 4 * r + j + 1)
                        if j == 0:
                            pe.wait_ge(s_vm, r + 1)
                        else:
                            pe.wait_ge(s_mpt, 4 * r + j)
                        for b in range(2):
                            for a in range(2):
                                mm = nc.tensor.transpose(MB[:, (2 * b + a) * P:(2 * b + a + 1) * P],
                                                         MP[:, j % 2, a, b * P:(b + 1) * P], ident[:, :])
                        mm.then_inc(s_mpT, 1)
                    return unit

                def values(half):
                    def unit():
                        pe.wait_ge(s_mpt, 4 * r + 2 * half + 2)
                        if half == 1:
                            pe.wait_ge(s_mo, 2 * r + 1)
                        for b in range(2):
                            mm = nc.tensor.matmul(OB[:, :], VM[:, b, :], PTM[:, b, half * HALF:(half + 1) * HALF],
                                                  start=(b == 0), stop=(b == 1))
                        mm.then_inc(s_mpv, 1)
                    return unit

                s, t, v = scores, turn, values
                return ({0: [v_turn], 1: [s(0)], 2: [s(1)], 4: [t(0)], 5: [s(2)], 6: [t(1)], 7: [s(3)]},
                        {1: [t(2)], 3: [v(0), t(3)], 5: [v(1)]})

            def mem_stage(base, layer, m, units):
                r = MH * layer + m
                tg, tq, tk, tv = (Tile(base, m, i) for i in range(4))
                first = isinstance(m, int) and m == 0
                if not first:
                    pe.wait_ge(s_km, r)
                tile(tg, units[0])
                if not first:
                    pe.wait_ge(s_tvm, r)
                tile(tq, units[1])
                pe.wait_ge(s_mgate, r + 1)
                if first:
                    pe.wait_ge(s_mlo, 4 * (layer + 1))
                mem_tile(tk)
                pe.wait_ge(s_mq, r + 1)
                mem_tile(tv)

            def mem_phase(base, layer):
                mem_prepare(layer)
                mem_stage(base, layer, 0, (None, None))
                with pe.Fori(1, MH) as m:
                    mem_stage(base, layer, m, mem_units(layer, m - 1))
                alone(mem_units(layer, MH - 1))

            def out_phase(base, layer):
                def one(s, i, ready=None):
                    t = Tile(base, s, i)
                    if not (isinstance(s, int) and s == 0 and i < 2):
                        pe.wait_ge(s_y, KB * layer + 4 * s + i - 1)
                    tile(t, rows=EB, lo=o_lo, ready=ready)

                def split(e):
                    pe.wait_ge(s_olo, EB * layer + e + 1)

                r = MH * (layer + 1)
                pe.wait_ge(s_km, r)
                pe.wait_ge(s_tvm, r)
                pe.wait_ge(s_wlo_x, layer + 1)
                one(0, 0, split)
                for i in range(1, 4):
                    one(0, i)
                with pe.Fori(1, KB // 4) as s:
                    for i in range(4):
                        one(s, i)
                pe.wait_ge(s_acc, KB * (layer + 1))
                for half in range(2):
                    mm = nc.tensor.matmul(SC[:, half, :], ones[:, :], O[:, 10, half * HALF:(half + 1) * HALF],
                                          start=True, stop=True)
                mm.then_inc(s_yss, 1)

            mem_phase(N_AM, 0)
            out_phase(N_AO, 0)
            for j in range(KB):
                pe.wait_ge(s_hsq, j + 1)
                if j == 0:
                    pe.wait_ge(s_rb, 1)
                for half in range(2):
                    mm = nc.tensor.matmul(SC[:, half, :], ones[:, :], O[:, 8 + j % 2, half * HALF:(half + 1) * HALF],
                                          start=(j == 0), stop=(j == KB - 1))
                mm.then_inc(s_hss, 1)

            pe.wait_ge(s_y, KB)
            tile(Tile(N_K, 0, 0), ready=lambda e: pe.wait_ge(s_xlo, KB + e + 1))
            tile(Tile(N_K, 0, 1))
            pe.wait_ge(s_rot, 1)
            tile(Tile(N_K, 0, 2))
            pe.wait_ge(s_rot, 2)
            tile(Tile(N_K, 0, 3))
            for i in range(2):
                pe.wait_ge(s_tvs, i + 1)
                for part in range(2):
                    if i or part:
                        pe.wait_ge(s_vs, 2 * i + part)
                    for c in range(4):
                        at = (4 * part + c) * P
                        mm = nc.tensor.transpose(MB[:, c * P:(c + 1) * P], T1[:, at:at + P] if i == 0 else RA[:, at:at + P],
                                                 ident[:, :])
                    mm.then_inc(s_vsT, 1)

            def swa_units(r):
                def scores(b):
                    def unit():
                        if b == 0:
                            pe.wait_ge(s_kp, 16 * 4 * (r + 1))
                            pe.wait_ge(s_rot, 2 + 2 * r + 2)
                        for p in range(2):
                            if b:
                                pe.wait_ge(s_msk, 16 * r + 2 * b + p - 1)
                            lo = P if b == 0 else 0
                            sc = SC[:, p, :].rearrange("q (h k) -> q h k", h=2)
                            mm = nc.tensor.matmul(sc[:, :, lo:2 * P], QR[:, p, b * P:(b + 1) * P],
                                                  KP[:, :, (b - 1) * P + lo:(b + 1) * P], start=True, stop=True)
                            mm.then_inc(s_sc, 1)
                    return unit

                def turn(b, k):
                    def unit():
                        pe.wait_ge(s_spn, CH * r + b + 1)
                        if b:
                            pe.wait_ge(s_spt, 15 * r + 2 * b - 1 + k)
                        for h in range(4):
                            mm = nc.tensor.transpose(MB[:, h * P:(h + 1) * P],
                                                     SM[:, b % 2, (2 * h + k) * P:(2 * h + k + 1) * P], ident[:, :])
                        mm.then_inc(s_spT, 1)
                    return unit

                def values(b):
                    def unit():
                        pe.wait_ge(s_spt, 15 * r + 2 * b + 1)
                        if b == 0:
                            pe.wait_ge(s_vg, r + 1)
                        else:
                            pe.wait_ge(s_so, CH * r + b)
                        blocks = (1,) if b == 0 else (0, 1)
                        for odd in range(2):
                            for k in blocks:
                                heads = PTS[:, k, odd:4:2, :]
                                mm = nc.tensor.matmul(OB[odd * DH:(odd + 1) * DH, 0:2 * P],
                                                      VG[:, b - 1 + k, :], heads, start=(k == blocks[0]), stop=(k == 1))
                        mm.then_inc(s_spv, 1)
                    return unit

                steps = [{}, {}, {}, {}]

                def put(k, unit):
                    steps[k // KB].setdefault(k % KB, []).append(unit)

                for i, k in enumerate(SWA_ROUNDS):
                    b = i - 2
                    if b > 0:
                        put(k, turn(b, 0))
                    if b >= 0:
                        put(k + 1, turn(b, 1))
                    if i < CH:
                        put(k + 1, scores(i))
                    if b >= 0:
                        put(min(k + 2, 4 * KB - 1), values(b))
                return steps

            def swa_stage(g, units):
                tiles = [Tile(N_S, g, i) for i in range(4)]
                pe.wait_ge(s_rot, 2 + 2 * g - 1) if not (isinstance(g, int) and g == 0) else pe.wait_ge(s_tvs, 1)
                tile(tiles[0], units[0])
                pe.wait_ge(s_rot, 2 + 2 * g) if not (isinstance(g, int) and g == 0) else pe.wait_ge(s_tvs, 2)
                tile(tiles[1], units[1])
                pe.wait_ge(s_sgate, 2 * g + 1)
                tile(tiles[2], units[2])
                pe.wait_ge(s_sgate, 2 * g + 2)
                tile(tiles[3], units[3])

            swa_stage(0, (None,) * 4)
            with pe.Fori(1, GROUPS) as g:
                swa_stage(g, swa_units(g - 1))
            alone(swa_units(GROUPS - 1))

            mem_phase(N_BM, 1)
            out_phase(N_BO, 1)
        @block.scalar
        def _(act):
            A = nc.scalar.activation

            def w_high(t, scaled=None, rows=slice(0, KB), extra=False):
                act.wait_ge(s_w_in[t.slot], 16 * (t.before + 1))
                if scaled is not None:
                    act.wait_ge(s_w_scaled, scaled)
                wait(act, s_mm, t.n - 1)
                A(w_hi[:, t.slot, rows, :], w_raw[:, t.slot, rows, :], ACT.Copy).then_inc(s_whi_x if extra else s_whi, 1)

            def sigmoid(z, tmp, steps, at, clamped, clamp_at):
                A(tmp, z, ACT.Exp, scale=-1.0).then_inc(steps, 1)
                act.wait_ge(clamped, clamp_at)
                A(tmp, tmp, ACT.Ln, bias=1.0).then_inc(steps, 1)
                act.wait_ge(steps, at + 2)
                A(tmp, tmp, ACT.Exp, scale=-1.0).then_inc(steps, 1)

            nc.scalar.preload_act_table_set("natural_log_exp_and_others")
            for e in range(KB):
                act.wait_ge(s_x_in[e], 16)
                if e >= 2:
                    act.wait_ge(s_xss, e - 1)
                A(KH[:, e % 2, :], O[:, e, :], ACT.Square).then_inc(s_xsq, 1)
            act.wait_ge(s_lbd, 1)
            A(lbt[:, :, :], lb2[:, :, :], ACT.Exp).then_inc(s_lb, 1)
            w_high(Tile(N_H, 0, 0))
            act.wait_ge(s_xss, KB)
            act.wait_ge(s_memset, 2)
            A(RB0[:, :], SCF, ACT.Ln, scale=1.0 / D, bias=eps_c[:, :]).then_inc(s_rnl, 1)
            act.wait_ge(s_rnl, 1)
            A(RB0[:, :], RB0[:, :], ACT.Exp, scale=-0.5).then_inc(s_rb0, 1)
            for e in range(KB):
                act.wait_ge(s_xs, e + 1)
                A(X[:, e, :], XS[:, e % 2, :], ACT.Copy).then_inc(s_xhi, 1)

            def hgrn_steps(r):
                def v_out():
                    act.wait_ge(s_mm, 4 * r + 4)
                    A(TV[:, :], Z[:, 1, :], ACT.Copy).then_inc(s_tv, 1)

                def v_copy(part):
                    act.wait_ge(s_vT, 2 * r + part + 1)
                    A(VN[:, part * HALF:(part + 1) * HALF], MB[:, :], ACT.Copy).then_inc(s_vn, 1)

                def level(l):
                    half = 1 << l
                    e = E2[:, l % 2, :].rearrange("p (n f i) -> p n f i", f=2, i=half)
                    act.wait_ge(s_dif, 8 * r + l + 1)
                    A(e[:, :, 0, :], e[:, :, 0, :], ACT.Exp, scale=-1.0)
                    A(e[:, :, 1, :], e[:, :, 1, :], ACT.Exp).then_inc(s_dec, 1)

                def q_decay():
                    act.wait_ge(s_hat, LEVELS * r + 6)
                    A(E2[:, 1, :], CUM[:, :], ACT.Exp).then_inc(s_dec, 1)
                    A(EL[:, :], CUM[:, P - 1:T:P], ACT.Exp).then_inc(s_el, 1)

                def k_decay():
                    act.wait_ge(s_dif, 8 * r + 8)
                    A(E2[:, 0, :], E2[:, 0, :], ACT.Exp).then_inc(s_dec, 1)

                def kd_copy(part):
                    act.wait_ge(s_kdT, 2 * r + part + 1)
                    A(KDT[:, part * HALF:(part + 1) * HALF], MB[:, :], ACT.Copy).then_inc(s_kdt, 1)

                def square(part):
                    act.wait_ge(s_fin, 2 * r + part + 1)
                    if part:
                        act.wait_ge(s_oss, 2 * r + 1)
                    A(SQ[:, :], OB[:, :], ACT.Square).then_inc(s_osq, 1)

                def inverse(part):
                    act.wait_ge(s_oss, 2 * r + part + 1)
                    if part:
                        act.wait_ge(s_on, 2 * r + 1)
                    A(RN[:, :], SC[:, part, :], ACT.Ln, scale=1.0 / P, bias=eps_c[:, :]).then_inc(s_rnl, 1)
                    act.wait_ge(s_rnl, 2 * r + part + 2)
                    A(RN[:, :], RN[:, :], ACT.Exp, scale=-0.5).then_inc(s_rn, 1)

                return v_out, v_copy, level, q_decay, k_decay, kd_copy, square, inverse

            def head_stage(h, project, attend):
                tiles = [Tile(N_H, h, i) for i in range(5)]
                if attend:
                    v_out, v_copy, level, q_decay, k_decay, kd_copy, square, inverse = hgrn_steps(h - 1)
                    level(0)
                    v_out()
                if project:
                    w_high(tiles[1])
                if attend:
                    level(1)
                    v_copy(0)
                    level(2)
                    v_copy(1)
                if project:
                    w_high(tiles[2])
                    act.wait_ge(s_mm, 4 * h + 1)
                    sigmoid(Z[:, 0, :], T1, s_sg, 10 * h, s_clamp, 3 * h + 1)
                if attend:
                    level(3)
                    level(4)
                    level(5)
                    level(6)
                    q_decay()
                if project:
                    w_high(tiles[3])
                    act.wait_ge(s_mm, 4 * h + 2)
                    act.wait_ge(s_silu, 2 * h + 1)
                    sigmoid(Z[:, 1, :], T1, s_sg, 10 * h + 3, s_clamp, 3 * h + 2)
                if attend:
                    k_decay()
                    kd_copy(0)
                    kd_copy(1)
                    square(0)
                if project:
                    w_high(Tile(N_H, h + 1, 0))
                    act.wait_ge(s_mm, 4 * h + 3)
                    act.wait_ge(s_silu, 2 * h + 2)
                    A(T1, Z[:, 0, :], ACT.Exp, scale=-1.0).then_inc(s_sg, 1)
                    act.wait_ge(s_clamp, 3 * h + 3)
                    A(T2, T1, ACT.Ln, bias=1.0).then_inc(s_sg, 1)
                    act.wait_ge(s_sg, 10 * h + 8)
                    A(T2, T2, ACT.Exp, scale=-1.0).then_inc(s_sg, 1)
                    act.wait_ge(s_k, h + 1)
                    A(T2, T2, ACT.Ln, scale=oml[:, bass.ds(h, 1)], bias=lb[:, bass.ds(h, 1)]).then_inc(s_sg, 1)
                if attend:
                    inverse(0)
                    square(1)
                    inverse(1)

            act.wait_ge(s_lb, 3)
            act.wait_ge(s_level, 1)
            head_stage(0, True, False)
            with act.Fori(1, HEADS) as h:
                head_stage(h, True, True)
            head_stage(HEADS, False, True)

            def mem_prepare(layer):
                act.wait_ge(s_mem_in, 16 * (layer + 1))
                for e in range(KB):
                    if e >= 2:
                        act.wait_ge(s_mss, KB * layer + e - 1)
                    A(MSQ[:, e % 2, :], MS[:, e, :], ACT.Square).then_inc(s_msq, 1)
                act.wait_ge(s_mss, KB * (layer + 1))
                A(RBM[:, :], MB[:, 0:MT], ACT.Ln, scale=1.0 / D, bias=eps_c[:, :]).then_inc(s_rbm, 1)
                act.wait_ge(s_rbm, 2 * layer + 1)
                A(RBM[:, :], RBM[:, :], ACT.Exp, scale=-0.5).then_inc(s_rbm, 1)
                for q4 in range(4):
                    act.wait_ge(s_mx, KB * layer + 2 * q4 + 2)
                    A(MHI[:, 2 * q4:2 * q4 + 2, :], MX[:, q4 % 2, :], ACT.Copy).then_inc(s_mhi, 1)

            def mem_attend(layer, m):
                r = MH * layer + m

                def v_copy():
                    act.wait_ge(s_vmT, r + 1)
                    A(VM[:, :, :], MB[:, 0:2 * P], ACT.Copy).then_inc(s_vm, 1)

                def exps(j):
                    act.wait_ge(s_mneg, 4 * r + j + 1)
                    for a in range(2):
                        e = A(MP[:, j % 2, a, :], SC[:, j % 2, a * MT:(a + 1) * MT], ACT.Exp, scale=MEM_SCALE,
                              bias=sm_neg[:, j % 2, a:a + 1], accum_out=sm_den[:, j % 2, a:a + 1])
                    e.then_inc(s_mexp, 1)

                def p_copy(j):
                    act.wait_ge(s_mpT, 4 * r + j + 1)
                    A(PTM[:, :, j * 2 * P:(j + 1) * 2 * P], MB[:, :], ACT.Copy).then_inc(s_mpt, 1)

                return v_copy, exps, p_copy

            def mem_stage(base, layer, m, project, attend, gain, last=False):
                r = MH * layer + m
                if attend:
                    v_copy, exps, p_copy = mem_attend(layer, m - 1)
                    act.wait_ge(s_mm, Tile(base, m, 0).n)
                    A(TVM[:, :], Z[:, 1, 0:MT], ACT.Copy).then_inc(s_tvm, 1)
                if project:
                    w_high(Tile(base, m, 1), 20 + 2 * m + 2 if gain else None)
                if attend:
                    v_copy()
                    exps(0)
                    exps(1)
                    p_copy(0)
                    exps(2)
                    p_copy(1)
                    exps(3)
                    p_copy(2)
                if project:
                    w_high(Tile(base, m, 2))
                    act.wait_ge(s_mm, Tile(base, m, 0).n + 1)
                    act.wait_ge(s_mlo, 4 * (layer + 1))
                    sigmoid(Z[:, 0, :], MT1[:, :], s_msg, 3 * r, s_mclamp, r + 1)
                if attend:
                    p_copy(3)
                if project:
                    w_high(Tile(base, m, 3))
                    act.wait_ge(s_mm, Tile(base, m, 1).n + 1)
                    A(MQ[:, :], Z[:, 1, :], ACT.Copy).then_inc(s_mq, 1)
                    if gain and not last:
                        w_high(Tile(base, m + 1, 0), 20 + 2 * m + 3)
                    else:
                        w_high(Tile(base, m + 1, 0))
                    act.wait_ge(s_mm, Tile(base, m, 2).n + 1)
                    A(KM[:, :], Z[:, 0, 0:MT], ACT.Copy).then_inc(s_km, 1)

            def mem_phase(base, layer):
                mem_prepare(layer)
                gain = layer == 1
                mem_stage(base, layer, 0, True, False, gain)
                with act.Fori(1, MH - gain) as m:
                    mem_stage(base, layer, m, True, True, gain)
                if gain:
                    mem_stage(base, layer, MH - 1, True, True, gain, last=True)
                mem_stage(base, layer, MH, False, True, gain)

            def out_phase(base, layer):
                w_high(Tile(base, 0, 0), rows=slice(KB, EB), extra=True)
                for e in range(EB):
                    if e == 0:
                        wait(act, s_mm, base)
                        if layer == 0:
                            act.wait_ge(s_on, 2 * HEADS)
                        else:
                            act.wait_ge(s_so, CH * GROUPS)
                    if e == KB:
                        act.wait_ge(s_mo, 2 * MH * (layer + 1))
                    A(X[:, e, :], O[:, e, :], ACT.Copy).then_inc(s_ohi, 1)

                def one(s, i, last=False):
                    t = Tile(base, s, i)
                    j = 4 * s + i
                    if not last:
                        w_high(Tile(base, s, i + 1) if i < 3 else Tile(base, s + 1, 0), rows=slice(0, EB))
                    act.wait_ge(s_mm, t.n + 1)
                    if not (isinstance(s, int) and s == 0 and i < 2):
                        act.wait_ge(s_acc, KB * layer + j - 1)
                    A(O[:, 8 + i % 2, :], Z[:, i % 2, :], ACT.Square).then_inc(s_ysq, 1)
                    A(O[:, j, :], Z[:, i % 2, :], ACT.Copy, scale=post_col[:, layer, j:j + 1]).then_inc(s_y, 1)

                act.wait_ge(s_olo, EB * (layer + 1))
                for i in range(4):
                    one(0, i)
                for i in range(4):
                    one(1, i, last=(i == 3))
                act.wait_ge(s_yss, layer + 1)
                A(RB[:, :], SCF, ACT.Ln, scale=1.0 / D, bias=eps_c[:, :])\
                    .then_inc(s_rbl, 1)
                act.wait_ge(s_rbl, layer + 1)
                A(RB[:, :], RB[:, :], ACT.Exp, scale=-0.5).then_inc(s_rb, 1)

            mem_phase(N_AM, 0)
            out_phase(N_AO, 0)
            for j in range(KB):
                act.wait_ge(s_h, j + 1)
                if j >= 2:
                    act.wait_ge(s_hss, j - 1)
                A(O[:, 8 + j % 2, :], O[:, j, :], ACT.Square).then_inc(s_hsq, 1)
            act.wait_ge(s_hss, KB)
            A(RB[:, :], SCF, ACT.Ln, scale=1.0 / D, bias=eps_c[:, :])\
                .then_inc(s_rb2l, 1)
            act.wait_ge(s_rb2l, 1)
            A(RB[:, :], RB[:, :], ACT.Exp, scale=-0.5).then_inc(s_rb2, 1)
            w_high(Tile(N_K, 0, 0), 1)
            for e in range(KB):
                act.wait_ge(s_hn, e + 1)
                A(X[:, e, :], XN[:, e % 2, :], ACT.Copy).then_inc(s_xhi, 1)
            w_high(Tile(N_K, 0, 1), 2)
            act.wait_ge(s_rtg, 1)
            A(rope_s[:, :], rope_s[:, :], ACT.Sin)
            A(rope_c[:, :], rope_c[:, :], ACT.Sin).then_inc(s_rope, 1)
            nc.scalar.preload_act_table_set("natural_log_exp_and_others")
            w_high(Tile(N_K, 0, 2), 3)
            w_high(Tile(N_K, 0, 3), 4)
            act.wait_ge(s_mm, N_K + 3)
            A(T1, Z[:, 0, :], ACT.Copy).then_inc(s_tvs, 1)
            w_high(Tile(N_S, 0, 0), 5)
            act.wait_ge(s_mm, N_K + 4)
            act.wait_ge(s_rot, 2)
            A(RA, Z[:, 1, :], ACT.Copy).then_inc(s_tvs, 1)
            for i in range(2):
                for part in range(2):
                    act.wait_ge(s_vsT, 2 * i + part + 1)
                    A(VALL[:, 4 * part:4 * part + 4, i * P:(i + 1) * P], MB[:, :], ACT.Copy).then_inc(s_vs, 1)

            def swa_attend(r):
                def exps(b):
                    lo = P if b == 0 else 0
                    sm = SM[:, b % 2, :].rearrange("p (h k) -> p h k", h=4)
                    act.wait_ge(s_sneg, CH * r + b + 1)
                    for h in range(4):
                        A(sm[:, h, lo:], sm[:, h, lo:], ACT.Exp, scale=SWA_SCALE, bias=sm_neg[:, b % 2, h:h + 1],
                          accum_out=sm_den[:, b % 2, h:h + 1])
                    A(sm_snk[:, b % 2, :], sm_snk[:, b % 2, :], ACT.Exp).then_inc(s_sexp, 1)

                def p_copy(b, k):
                    act.wait_ge(s_spT, 15 * r + (2 * b + k if b else 1))
                    if b:
                        act.wait_ge(s_spv, CH * r + b)
                    A(PTS[:, k, :, :], MB[:, :], ACT.Copy).then_inc(s_spt, 1)

                return exps, p_copy

            def swa_stage(g, project, attend):
                tiles = [Tile(N_S, g, i) for i in range(4)]
                if attend:
                    exps, p_copy = swa_attend(g - 1)

                def rounds(i0, i1):
                    for i in range(i0, i1):
                        b = i - 2
                        if b > 0:
                            p_copy(b, 0)
                        if b >= 0:
                            p_copy(b, 1)
                        if i < CH:
                            exps(i)

                def gate(i):
                    act.wait_ge(s_mm, tiles[i].n + 1)
                    wait(act, s_sgate, 2 * g + i)
                    sigmoid(Z[:, i, :], T1, s_ssg, 6 * g + 3 * i, s_sclamp, 2 * g + i + 1)

                scaled = 4 + 4 * g
                if project:
                    w_high(tiles[1], scaled + 2)
                if attend:
                    rounds(0, 1)
                if project:
                    w_high(tiles[2], scaled + 3)
                    gate(0)
                if attend:
                    rounds(1, 4)
                if project:
                    w_high(tiles[3], scaled + 4)
                    gate(1)
                if attend:
                    rounds(4, CH)
                if project:
                    w_high(Tile(N_S, g + 1, 0), scaled + 5)
                if attend:
                    rounds(CH, CH + 2)
                if project:
                    if isinstance(g, int) and g == 0:
                        act.wait_ge(s_vs, 4)
                    else:
                        act.wait_ge(s_spv, CH * g)
                    A(VG[:, :, :], VALL[:, :, bass.ds(g * DH, DH)], ACT.Copy).then_inc(s_vg, 1)

            swa_stage(0, True, False)
            with act.Fori(1, GROUPS) as g:
                swa_stage(g, True, True)
            swa_stage(GROUPS, False, True)
            mem_phase(N_BM, 1)
            out_phase(N_BO, 1)
        @block.vector
        def _(dve):
            TT = nc.vector.tensor_tensor
            STT = nc.vector.scalar_tensor_tensor
            TS = nc.vector.tensor_scalar

            def w_low(t, rows=slice(0, KB), extra=False):
                dve.wait_ge(s_whi_x if extra else s_whi, (1 + (t.n > N_AO)) if extra else t.n + 1)
                TT(w_lo[:, t.slot, rows, :], w_raw[:, t.slot, rows, :], w_hi[:, t.slot, rows, :].bitcast(F32),
                   ALU.subtract).then_inc(s_wlo_x if extra else s_wlo, 1)

            nc.vector.memset(ones[:, :], 1.0).then_inc(s_memset, 1)
            nc.vector.memset(eps_c[:, :], EPS).then_inc(s_memset, 1)
            dve.wait_ge(s_const, 16 * (N_CONST - 1))
            nc.vector.tensor_copy(level_mask[:, :, :], LMF).then_inc(s_level, 1)
            TT(lb[:, :], lb2[:, 0, :], lb2[:, 1, :], ALU.max).then_inc(s_memset, 1)
            dve.wait_ge(s_memset, 3)
            TT(lb2[:, :, :], lb2[:, :, :], bc(lb[:, :], 2), ALU.subtract).then_inc(s_lbd, 1)
            dve.wait_ge(s_lb, 1)
            TT(lb[:, :], lbt[:, 0, :], lbt[:, 1, :], ALU.add).then_inc(s_lbd, 1)
            dve.wait_ge(s_lbd, 2)
            nc.vector.reciprocal(lb[:, :], lb[:, :]).then_inc(s_lbd, 1)
            dve.wait_ge(s_lbd, 3)
            TT(oml[:, :], lb[:, :], lbt[:, 1, :], ALU.mult).then_inc(s_lb, 1)
            TT(lb[:, :], lb[:, :], lbt[:, 0, :], ALU.mult).then_inc(s_lb, 1)
            w_low(Tile(N_H, 0, 0))
            dve.wait_ge(s_rb0, 1)
            for e in range(KB):
                STT(XS[:, e % 2, :], O[:, e, :], pre_col[:, 0, e:e + 1], RB0[:, :], ALU.mult, ALU.mult)\
                    .then_inc(s_xs, 1)
                dve.wait_ge(s_xhi, e + 1)
                dve.wait_ge(s_xs, e + 1)
                TT(X[:, 8 + e, :], XS[:, e % 2, :], X[:, e, :].bitcast(F32), ALU.subtract).then_inc(s_xlo, 1)

            def clamp(tmp, steps, at, sem_):
                dve.wait_ge(steps, at)
                TS(tmp, tmp, BIG, None, ALU.min).then_inc(sem_, 1)

            def hgrn_steps(r):
                def dif(l):
                    half = 1 << l
                    e = E2[:, l % 2, :].rearrange("p (n b) -> p n b", b=2 * half)
                    c = CUM[:, :].rearrange("p (n b) -> p n b", b=2 * half)
                    if l == 0:
                        dve.wait_ge(s_cum, r + 1)
                    if l >= 2:
                        dve.wait_ge(s_hat, LEVELS * r + l - 1)
                    TT(e, c, c[:, :, half - 1:half].to_broadcast([P, T // (2 * half), 2 * half]), ALU.subtract)\
                        .then_inc(s_dif, 1)

                def dif_end():
                    dve.wait_ge(s_hat, LEVELS * r + LEVELS)
                    c = CUM[:, :].rearrange("p (n b) -> p n b", b=P)
                    TT(E2[:, 0, :].rearrange("p (n b) -> p n b", b=P), c[:, :, P - 1:P].to_broadcast([P, CH, P]), c,
                       ALU.subtract).then_inc(s_dif, 1)

                def diagonal(part):
                    dve.wait_ge(s_diag, 2 * r + part + 1)
                    TT(PT[:, part * HALF:(part + 1) * HALF].rearrange("p (c t) -> p c t", c=4),
                       SC[:, part, :].rearrange("p (c t) -> p c t", c=4), bc(ident[:, :], 4), ALU.mult)\
                        .then_inc(s_diag_ev, 1)

                def merge(l):
                    half = 1 << l
                    if l == 0:
                        dve.wait_ge(s_diag_ev, 2 * r + 2)
                    else:
                        dve.wait_ge(s_pred, LEVELS * r + l)
                    dve.wait_ge(s_lev, LEVELS * r + l + 1)
                    nc.vector.memset(pad[:, :], 0.0)
                    nc.vector.copy_predicated(
                        PT[:, :].rearrange("p (n f i) -> p n f i", f=2, i=half)[:, :, 1, :],
                        level_mask[:, l, :].rearrange("p (n i) -> p n i", i=half),
                        SC[:, l % 2, :].rearrange("p (n i) -> p n i", i=half)).then_inc(s_pred, 1)

                def state(c):
                    dve.wait_ge(s_stm, (CH - 1) * r + c + 1)
                    st = MB[:, 0:P]
                    if c == 0:
                        i = nc.vector.tensor_copy(ST[:, 1, :], st)
                    else:
                        dve.wait_ge(s_el, r + 1)
                        dve.wait_ge(s_st, (CH - 1) * r + c)
                        i = STT(ST[:, (c + 1) % 2, :], ST[:, c % 2, :], EL[:, c:c + 1], st, ALU.mult, ALU.add)
                    i.then_inc(s_st, 1)

                def gate(part):
                    o = O[:, bass.ds(r, 1), part * HALF:(part + 1) * HALF]
                    dve.wait_ge(s_osq, 2 * r + part + 1)
                    STT(o, OB[:, :].unsqueeze(1), out_col[:, bass.ds(r, 1)], o, ALU.mult, ALU.mult).then_inc(s_og, 1)

                return dif, dif_end, diagonal, merge, state, gate

            def head_stage(h, project, attend):
                if attend:
                    dif, dif_end, diagonal, merge, state, gate = hgrn_steps(h - 1)
                if project:
                    w_low(Tile(N_H, h, 1))
                if attend:
                    diagonal(0)
                    diagonal(1)
                    dif(2)
                    merge(0)
                    dif(3)
                    merge(1)
                if project:
                    w_low(Tile(N_H, h, 2))
                    clamp(T1, s_sg, 10 * h + 1, s_clamp)
                    dve.wait_ge(s_sg, 10 * h + 3)
                    TT(Q[:, bass.ds(h % 2, 1), :], Z[:, 0:1, :], T1.unsqueeze(1), ALU.mult).then_inc(s_silu, 1)
                if attend:
                    dif(4)
                    merge(2)
                    dif(5)
                    merge(3)
                    dif(6)
                    merge(4)
                    dif_end()
                if project:
                    w_low(Tile(N_H, h, 3))
                    clamp(T1, s_sg, 10 * h + 4, s_clamp)
                    dve.wait_ge(s_sg, 10 * h + 6)
                    TT(O[:, bass.ds(h, 1), :], Z[:, 1:2, :], T1.unsqueeze(1), ALU.mult).then_inc(s_silu, 1)
                if attend:
                    merge(5)
                    merge(6)
                    for c in range(4):
                        state(c)
                    gate(0)
                if project:
                    w_low(Tile(N_H, h + 1, 0))
                if attend:
                    state(4)
                if project:
                    clamp(T1, s_sg, 10 * h + 7, s_clamp)
                if attend:
                    state(5)
                if project:
                    dve.wait_ge(s_sg, 10 * h + 9)
                    dve.wait_ge(s_clamp, 3 * h + 3)
                    STT(KK[:, :], T1, oml[:, bass.ds(h, 1)], T2, ALU.mult, ALU.mult).then_inc(s_k, 1)
                if attend:
                    state(6)
                if project:
                    dve.wait_ge(s_sg, 10 * h + 10)
                    for c in range(CH):
                        i = nc.vector.tensor_tensor_scan(CUM[:, c * P:(c + 1) * P], ones[:, :], T2[:, c * P:(c + 1) * P],
                                                         0.0, ALU.mult, ALU.add)
                    i.then_inc(s_cum, 1)
                    next_dif = hgrn_steps(h)[0]
                    next_dif(0)
                    next_dif(1)
                if attend:
                    gate(1)

            head_stage(0, True, False)
            with dve.Fori(1, HEADS) as h:
                head_stage(h, True, True)
            head_stage(HEADS, False, True)

            def mem_prepare(layer):
                dve.wait_ge(s_rbm, 2 * layer + 2)
                for e in range(KB):
                    STT(MX[:, (e // 2) % 2, (e % 2) * MT:(e % 2 + 1) * MT], MS[:, e, :], mem_col[:, layer, e:e + 1],
                        RBM[:, :], ALU.mult, ALU.mult).then_inc(s_mx, 1)
                    if e % 2:
                        dve.wait_ge(s_mhi, 4 * layer + e // 2 + 1)
                        dve.wait_ge(s_mx, KB * layer + e + 1)
                        TT(MLO[:, e - 1:e + 1, :], MX[:, (e // 2) % 2, :].rearrange("p (a t) -> p a t", a=2),
                           MHI[:, e - 1:e + 1, :].bitcast(F32), ALU.subtract).then_inc(s_mlo, 1)

            def mem_attend(layer, m):
                r = MH * layer + m

                def maximum(j):
                    dve.wait_ge(s_msc, 4 * r + j + 1)
                    nc.vector.tensor_reduce(sm_max[:, j % 2, 0:2], SC[:, j % 2, :].rearrange("p (a m) -> p a m", a=2),
                                            AX.X, ALU.max).then_inc(s_mmax, 1)
                    dve.wait_ge(s_mmax, 4 * r + j + 1)
                    TS(sm_neg[:, j % 2, 0:2], sm_max[:, j % 2, 0:2], -MEM_SCALE, None, ALU.mult).then_inc(s_mneg, 1)

                def normalise(j):
                    dve.wait_ge(s_mexp, 4 * r + j + 1)
                    nc.vector.reciprocal(sm_inv[:, j % 2, 0:2], sm_den[:, j % 2, 0:2]).then_inc(s_minv, 1)
                    dve.wait_ge(s_minv, 4 * r + j + 1)
                    for a in range(2):
                        i = TS(MP[:, j % 2, a, :], MP[:, j % 2, a, :], sm_inv[:, j % 2, a:a + 1], None, ALU.mult)
                    i.then_inc(s_mpn, 1)

                def gate(half):
                    dve.wait_ge(s_mpv, 2 * r + half + 1)
                    o = O[:, bass.ds(m + 8, 1), half * HALF:(half + 1) * HALF]
                    TT(o, OB[:, :].unsqueeze(1), o, ALU.mult).then_inc(s_mo, 1)

                return maximum, normalise, gate

            def mem_stage(base, layer, m, project, attend):
                r = MH * layer + m
                if attend:
                    maximum, normalise, gate = mem_attend(layer, m - 1)
                    maximum(0)
                if project:
                    w_low(Tile(base, m, 1))
                if attend:
                    maximum(1)
                    normalise(0)
                    maximum(2)
                    normalise(1)
                    maximum(3)
                    normalise(2)
                if project:
                    w_low(Tile(base, m, 2))
                    clamp(MT1[:, :], s_msg, 3 * r + 1, s_mclamp)
                    dve.wait_ge(s_msg, 3 * r + 3)
                    TT(O[:, bass.ds(m + 8, 1), :], Z[:, 0:1, :], MT1[:, :].unsqueeze(1), ALU.mult).then_inc(s_mgate, 1)
                if attend:
                    normalise(3)
                    gate(0)
                    gate(1)
                if project:
                    w_low(Tile(base, m, 3))
                    w_low(Tile(base, m + 1, 0))

            def rope_tables():
                at = [0]

                def link(i):
                    at[0] += 1
                    i.then_inc(s_rt, 1)
                    dve.wait_ge(s_rt, at[0])

                dve.wait_ge(s_pos, 16)
                ang, k, r = RTA[:, :], RTB[:, :], RTC[:, :]
                link(nc.vector.tensor_copy(r, RTP[:, :]))
                link(TS(ang, r, freq[:, 0:1], None, ALU.mult))
                link(TS(k, ang, 1.0 / (2 * PI), None, ALU.mult))
                link(nc.vector.tensor_copy(RTP[:, :], k))
                link(nc.vector.tensor_copy(k, RTP[:, :]))
                c1 = 6.28125
                c2 = float(np.float32(np.round((2 * np.pi - c1) * 2 ** 22) / 2 ** 22))
                c3 = float(2 * np.pi - c1 - c2)
                for c in (c1, c2, c3):
                    link(STT(ang, k, -c, ang, ALU.mult, ALU.add))
                link(TS(k, ang, PI, -2 * PI, ALU.is_gt, ALU.mult))
                link(TT(ang, ang, k, ALU.add))
                link(TS(k, ang, -PI, 2 * PI, ALU.is_lt, ALU.mult))
                link(TT(ang, ang, k, ALU.add))
                top = 3.1415925
                link(TS(rope_s[:, :], ang, top, -top, ALU.min, ALU.max))
                link(TS(ang, ang, PI / 2, None, ALU.add))
                link(TS(k, ang, PI, -2 * PI, ALU.is_gt, ALU.mult))
                link(TT(ang, ang, k, ALU.add))
                TS(rope_c[:, :], ang, top, -top, ALU.min, ALU.max).then_inc(s_rtg, 1)

            def mem_phase(base, layer):
                mem_prepare(layer)
                mem_stage(base, layer, 0, True, False)
                with dve.Fori(1, MH) as m:
                    mem_stage(base, layer, m, True, True)
                mem_stage(base, layer, MH, False, True)

            def out_phase(base, layer):
                w_low(Tile(base, 0, 0), rows=slice(KB, EB), extra=True)
                for e in range(EB):
                    dve.wait_ge(s_ohi, EB * layer + e + 1)
                    lo = X[:, 12 + e, :] if e < 4 else OLO[:, e - 4, :]
                    TT(lo, O[:, e, :], X[:, e, :].bitcast(F32), ALU.subtract).then_inc(s_olo, 1)
                for j in range(1, KB):
                    w_low(Tile(base, j // 4, j % 4), rows=slice(0, EB))
                dve.wait_ge(s_rb, layer + 1)
                for j in range(KB):
                    TT(O[:, j, :], O[:, j, :], RB[:, :], ALU.mult).then_inc(s_yn, 1)
                    dve.wait_ge(s_yn, KB * layer + j + 1)
                    dve.wait_ge(s_hr[j % 2], 16 * (4 * layer + j // 2 + 1))
                    TT(O[:, j, :], O[:, j, :], HR[:, j % 2, :], ALU.add).then_inc(s_h, 1)

            mem_phase(N_AM, 0)
            out_phase(N_AO, 0)
            dve.wait_ge(s_rb2, 1)
            for e in range(KB):
                TT(XN[:, e % 2, :], O[:, e, :], RB[:, :], ALU.mult).then_inc(s_hn, 1)
                if e == 0:
                    w_low(Tile(N_K, 0, 0))
                dve.wait_ge(s_xhi, KB + e + 1)
                TT(X[:, 8 + e, :], XN[:, e % 2, :], X[:, e, :].bitcast(F32), ALU.subtract).then_inc(s_xlo, 1)

            def rotate(slot, before, to, ra):
                z = Z[:, slot, :]
                wait(dve, s_rot, before)
                TT(ra, z, rope_c[:, :], ALU.mult).then_inc(s_ra, 1)
                TT(z, z, rope_s[:, :], ALU.mult).then_inc(s_ra, 1)
                dve.wait_ge(s_ra, 2 * (before + 1))
                TT(to[0:64, :], ra[0:64, :], Z[64:128, slot, :], ALU.subtract)
                TT(to[64:128, :], ra[64:128, :], Z[0:64, slot, :], ALU.add).then_inc(s_rot, 1)

            rope_tables()
            dve.wait_ge(s_rope, 1)
            for i in range(2):
                w_low(Tile(N_K, 0, i + 1))
                dve.wait_ge(s_mm, N_K + i + 1)
                rotate(i, i, KST[:, i, :], RA)
            w_low(Tile(N_K, 0, 3))
            w_low(Tile(N_S, 0, 0))

            def swa_attend(r):
                def mask(b):
                    lo = P if b == 0 else 0
                    sm = SM[:, b % 2, :].rearrange("p (h k) -> p h k", h=4)
                    if b >= 2:
                        dve.wait_ge(s_spT, 15 * r + 2 * (b - 2) + 1)
                    for p in range(2):
                        dve.wait_ge(s_sc, 16 * r + 2 * b + p + 1)
                        TT(sm[:, 2 * p:2 * p + 2, lo:], SC[:, p, :].rearrange("p (h k) -> p h k", h=2)[:, :, lo:],
                           bc(window[:, lo:], 2), ALU.add).then_inc(s_msk, 1)
                    dve.wait_ge(s_msk, 16 * r + 2 * b + 2)
                    nc.vector.tensor_reduce(sm_max[:, b % 2, :], sm[:, :, lo:], AX.X, ALU.max).then_inc(s_smax, 1)
                    dve.wait_ge(s_smax, CH * r + b + 1)
                    sink = sink_b[:, bass.ds(4 * r, 4)]
                    STT(sm_max[:, b % 2, :], sm_max[:, b % 2, :], SWA_SCALE, sink, ALU.mult, ALU.max).then_inc(s_sm, 1)
                    dve.wait_ge(s_sm, 2 * (CH * r + b) + 1)
                    TT(sm_snk[:, b % 2, :], sink, sm_max[:, b % 2, :], ALU.subtract).then_inc(s_sm, 1)
                    TS(sm_neg[:, b % 2, :], sm_max[:, b % 2, :], -1.0, None, ALU.mult).then_inc(s_sneg, 1)

                def normalise(b):
                    lo = P if b == 0 else 0
                    sm = SM[:, b % 2, :].rearrange("p (h k) -> p h k", h=4)
                    dve.wait_ge(s_sexp, CH * r + b + 1)
                    TT(sm_den[:, b % 2, :], sm_den[:, b % 2, :], sm_snk[:, b % 2, :], ALU.add).then_inc(s_sden, 1)
                    dve.wait_ge(s_sden, CH * r + b + 1)
                    nc.vector.reciprocal(sm_inv[:, b % 2, :], sm_den[:, b % 2, :]).then_inc(s_sinv, 1)
                    dve.wait_ge(s_sinv, CH * r + b + 1)
                    for h in range(4):
                        i = TS(sm[:, h, lo:], sm[:, h, lo:], sm_inv[:, b % 2, h:h + 1], None, ALU.mult)
                    i.then_inc(s_spn, 1)

                def gate(b):
                    dve.wait_ge(s_spv, CH * r + b + 1)
                    o = O[:, bass.ds(2 * r, 2), b * P:(b + 1) * P]
                    TT(o, OB[:, 0:2 * P].rearrange("p (a t) -> p a t", a=2), o,
                       ALU.mult).then_inc(s_so, 1)

                return mask, normalise, gate

            def swa_stage(g, project, attend):
                if attend:
                    mask, normalise, gate = swa_attend(g - 1)

                def rounds(i0, i1):
                    for i in range(i0, i1):
                        if 1 <= i <= CH:
                            normalise(i - 1)
                        if i < CH:
                            mask(i)
                        if i >= 2:
                            gate(i - 2)

                def silu(i):
                    clamp(T1, s_ssg, 6 * g + 3 * i + 1, s_sclamp)
                    dve.wait_ge(s_ssg, 6 * g + 3 * i + 3)
                    TT(O[:, bass.ds(2 * g + i, 1), :], Z[:, i:i + 1, :], T1.unsqueeze(1), ALU.mult).then_inc(s_sgate, 1)

                if attend:
                    dve.wait_ge(s_mm, Tile(N_S, g, 0).n)
                    rotate(1, 2 + 2 * (g - 1) + 1, QR[:, 1, :], RA)
                if project:
                    w_low(Tile(N_S, g, 1))
                if attend:
                    rounds(0, 1)
                if project:
                    w_low(Tile(N_S, g, 2))
                    silu(0)
                if attend:
                    rounds(1, 4)
                if project:
                    w_low(Tile(N_S, g, 3))
                    silu(1)
                if attend:
                    rounds(4, CH)
                if project:
                    w_low(Tile(N_S, g + 1, 0))
                    dve.wait_ge(s_mm, Tile(N_S, g, 2).n + 1)
                    rotate(0, 2 + 2 * g, QR[:, 0, :], RA)
                if attend:
                    rounds(CH, CH + 2)

            swa_stage(0, True, False)
            with dve.Fori(1, GROUPS) as g:
                swa_stage(g, True, True)
            swa_stage(GROUPS, False, True)
            mem_phase(N_BM, 1)
            out_phase(N_BO, 1)

        @block.gpsimd
        def _(pool):
            GT = nc.gpsimd.tensor_tensor
            pool.wait_ge(s_xss, KB)
            nc.gpsimd.memset(KH[:, :, :], 0.0).then_inc(s_kz, 1)
            pool.wait_ge(s_kz, 1)

            def hgrn(r):
                q1 = Q[:, bass.ds(r % 2, 1), :].rearrange("p a t -> p (a t)")
                pool.wait_ge(s_silu, 2 * r + 1)
                for l in range(LEVELS):
                    half = 1 << l

                    def halves(ap):
                        return ap.rearrange("p (n f i) -> p n f i", f=2, i=half)

                    e = halves(E2[:, l % 2, :])
                    pool.wait_ge(s_dec, 9 * r + l + 1)
                    if l >= 2:
                        pool.wait_ge(s_lev, LEVELS * r + l - 1)
                    GT(halves(KH[:, l % 2, :])[:, :, 0, :], halves(KK[:, :])[:, :, 0, :], e[:, :, 0, :], ALU.mult)
                    GT(QH[:, l % 2, :].rearrange("p (n i) -> p n i", i=half), halves(q1)[:, :, 1, :], e[:, :, 1, :],
                       ALU.mult).then_inc(s_hat, 1)
                pool.wait_ge(s_dec, 9 * r + 8)
                pool.wait_ge(s_diag, 2 * r + 2)
                pool.wait_ge(s_hat, LEVELS * (r + 1))
                GT(q1, q1, E2[:, 1, :], ALU.mult).then_inc(s_qc, 1)
                pool.wait_ge(s_dec, 9 * r + 9)
                GT(E2[:, 0, :], KK[:, :], E2[:, 0, :], ALU.mult).then_inc(s_kd, 1)
                for part in range(2):
                    o = O[:, bass.ds(r, 1), part * HALF:(part + 1) * HALF]
                    pool.wait_ge(s_rn, 2 * r + part + 1)
                    pool.wait_ge(s_og, 2 * r + part + 1)
                    GT(o, o, RN[:, :].unsqueeze(1), ALU.mult).then_inc(s_on, 1)

            hgrn(0)
            with pool.Fori(1, HEADS) as r:
                hgrn(r)

            def load_memory(layer):
                if layer == 0:
                    pool.wait_ge(s_on, 2 * HEADS)
                else:
                    pool.wait_ge(s_so, CH * GROUPS)
                pool.dma_start(MS[:, :, :], mem).then_inc(s_mem_in, 16)

            def out_phase(base, layer):
                acc = O[:, 10, :]
                for j in range(KB):
                    pool.wait_ge(s_ysq, KB * layer + j + 1)
                    if j == 0:
                        nc.gpsimd.tensor_copy(acc, O[:, 8, :]).then_inc(s_acc, 1)
                    else:
                        pool.wait_ge(s_acc, KB * layer + j)
                        GT(acc, acc, O[:, 8 + j % 2, :], ALU.add).then_inc(s_acc, 1)
                for j in range(KB):
                    if j == 0:
                        pool.wait_ge(s_mm, base + KB)
                    if j >= 2:
                        pool.wait_ge(s_h, KB * layer + j - 1)
                    pool.dma_start(HR[:, j % 2, :], (x if layer == 0 else h_dram)[:, j, :]).then_inc(s_hr[j % 2], 16)

            load_memory(0)
            out_phase(N_AO, 0)
            for j in range(KB):
                pool.wait_ge(s_h, j + 1)
                pool.dma_start(h_dram[:, j, :], O[:, j, :]).then_inc(s_h_out[j % 2], 16)

            scaled = [0]

            def scale(t, col):
                pool.wait_ge(s_w_in[t.slot], 16 * (t.before + 1))
                w = w_raw[:, t.slot, 0:KB, :]
                GT(w, w, col.unsqueeze(2).to_broadcast([P, KB, P]), ALU.mult).then_inc(s_w_scaled, 1)

            scale(Tile(N_K, 0, 0), kv_col[:, :])
            pool.dma_start(RTP[:, :], positions.to_broadcast([P, T])).then_inc(s_pos, 16)
            for i in range(1, 4):
                scale(Tile(N_K, 0, i), kv_col[:, :])
            scale(Tile(N_S, 0, 0), pre_col[:, 1, :])
            for i in range(2):
                pool.wait_ge(s_rot, i + 1)
                for f in range(2):
                    for hh in range(2):
                        pool.dma_start(k_dram[2 * i + hh, f], KST[64 * f + 32 * hh:64 * f + 32 * hh + 32, i, :])\
                            .then_inc(s_k_out, 16)
            nc.gpsimd.memset(KP[:, :, :], 0.0).then_inc(s_kz, 1)
            pool.wait_ge(s_kz, 2)
            pool.wait_ge(s_k_out, 16 * 8)

            def swa(g, first=False):
                for i in range(1, 4):
                    scale(Tile(N_S, g, i), pre_col[:, 1, :])
                scale(Tile(N_S, g + 1, 0), pre_col[:, 1, :])
                if not first:
                    pool.wait_ge(s_sc, 16 * g)
                for odd in range(2):
                    for f in range(2):
                        at = 64 * f + 32 * odd
                        pool.dma_start(KP[at:at + 32, odd, :], k_dram[bass.ds(g, 1), f].rearrange("a i t -> (a i) t"))\
                            .then_inc(s_kp, 16)

            swa(0, True)
            with pool.Fori(1, GROUPS) as g:
                swa(g)
            load_memory(1)
            def mem_scale(m):
                scale(Tile(N_BM, m, 1), pre_col[:, 1, :])
                scale(Tile(N_BM, m + 1, 0), pre_col[:, 1, :])

            mem_scale(0)
            with pool.Fori(1, MH - 1) as m:
                mem_scale(m)
            scale(Tile(N_BM, MH - 1, 1), pre_col[:, 1, :])
            out_phase(N_BO, 1)
            for j in range(KB):
                pool.wait_ge(s_h, KB + j + 1)
                pool.dma_start(out[:, j, :], O[:, j, :]).then_inc(s_out[j % 2], 16)
            for s in s_out:
                pool.wait_ge(s, 16 * KB // 2)
            for s in s_h_out:
                pool.wait_ge(s, 16 * KB // 2)


def constants():
    ident = np.eye(P, dtype=np.float32)
    s = np.arange(P)[:, None]
    level = np.zeros((P, LEVELS, CH, P // 2), np.float32)
    for l in range(LEVELS):
        half = 1 << l
        t = np.arange(P).reshape(-1, 2, half)[:, 1, :].reshape(1, -1)
        level[:, l] = ((s // (2 * half) == t // (2 * half)) & (s // half % 2 == 0))[:, None, :]
    q = np.arange(P)[:, None]
    k = np.arange(2 * P)[None, :]
    window = np.where((k > q) & (k <= q + P), 0.0, NEG).astype(np.float32)
    i = np.arange(P) % (DH // 2)
    freq = (10000.0 ** (-2.0 * i / DH)).astype(np.float32).reshape(P, 1)
    return {"c_ident": ident, "c_level": level.reshape(P, LEVELS, HALF), "c_window": window, "c_freq": freq}


def _tiles(w):
    return w.reshape(-1, P, w.shape[1] // P, P).transpose(2, 1, 0, 3)


def _columns(v):
    v = v.reshape(v.shape[:-1] + (-1, P))
    return np.moveaxis(v, -1, 0)


def _rotary(w):
    return w.reshape(w.shape[0], -1, 2, 2, DH // 2).transpose(0, 1, 3, 2, 4).reshape(w.shape)


def _features(a):
    return a.T.reshape(-1, P, a.shape[0]).transpose(1, 0, 2)


def _layout(i):
    b = i["b_w_in"][0]
    kv = i["w_kv_shared"]
    return [
        ("x", _features(i["x"][0])), ("mem", _features(i["mem"][0])), ("positions", i["positions"]),
        ("pre", _columns(i["pre_norm_g"])), ("post", _columns(i["post_norm_g"])), ("memg", _columns(i["mem_norm_g"])),
        ("wmem", np.concatenate([_tiles(w) for w in i["w_mem_kv"]])), ("awin", _tiles(i["a_w_in"][0])),
        ("lb", _columns(i["a_lb_logits"])), ("outg", _columns(i["a_out_norm_g"][0])), ("awout", _tiles(i["a_w_out"][0])),
        ("kvg", _columns(i["kv_norm_g"])),
        ("wkv", _tiles(np.concatenate([_rotary(kv[:, :GROUPS * DH]), kv[:, GROUPS * DH:]], 1))),
        ("bwin", _tiles(np.concatenate([_rotary(b[:, :D]), b[:, D:]], 1))),
        ("sinks", i["b_sinks"]), ("bwout", _tiles(i["b_w_out"][0])),
    ]


def kernel(**inputs):
    import concourse.bacc as bacc
    from concourse.bass_utils import run_bass_kernel_spmd as run

    nc = bacc.Bacc("TRN2", target_bir_lowering=False, num_devices=1)
    arrays, args = {}, []
    for name, a in _layout({n: np.asarray(a) for n, a in inputs.items()}) + list(constants().items()):
        a = np.ascontiguousarray(a)
        arrays[f"in_{name}"] = a
        args.append(nc.dram_tensor(f"in_{name}", a.shape, mybir.dt.from_np(a.dtype), kind="ExternalInput").ap())
    args.append(nc.dram_tensor("h_scratch", (P, KB, T), F32, kind="Internal").ap())
    args.append(nc.dram_tensor("k_scratch", (GROUPS, 2, DH // 2, T), F32, kind="Internal").ap())
    args.append(nc.dram_tensor("out_0", (P, KB, T), F32, kind="ExternalOutput").ap())
    build(nc, *args)
    r = run(nc, [arrays], core_ids=[0])
    return np.ascontiguousarray(r.results[0]["out_0"].transpose(2, 1, 0).reshape(1, T, D))
```

```python
from contextlib import ExitStack

import numpy as np

import concourse.bass as bass
from concourse import mybir

F32 = mybir.dt.float32
F32R = mybir.dt.float32r
I32 = mybir.dt.int32
U8 = mybir.dt.uint8
ACT = mybir.ActivationFunctionType
ALU = mybir.AluOpType
AX = mybir.AxisListType

P = 128
D = 1024
T = 1024
KB = D // P
HALF = 512
HEADS = 8
CH = T // P
LEVELS = 7
MT = 256
MH = 4
EB = 12
GROUPS = 4
DH = 64
EPS = 1e-6
BIG = float(2.0 ** 62)
MEM_SCALE = float(P) ** -0.5
SWA_SCALE = float(DH) ** -0.5
NEG = -1e38
PI = float(np.pi)

N_H = 0
N_AM = N_H + 4 * HEADS
N_AO = N_AM + 4 * MH
N_K = N_AO + KB
N_S = N_K + 4
N_BM = N_S + 4 * GROUPS
N_BO = N_BM + 4 * MH

SWA_ROUNDS = (4, 6, 9, 12, 15, 18, 20, 23, 26, 29)
SWA_LAST_ROUNDS = (3, 4, 6, 8, 9, 11, 12, 14, 16, 18)


class Tile:

    def __init__(self, base, stage, i):
        self.slot = i % 2
        self.n = base + 4 * stage + i
        self.before = base // 2 + 2 * stage + i // 2


def wait(eng, semaphore, value):
    if not (isinstance(value, int) and value <= 0):
        eng.wait_ge(semaphore, value)


def build(nc, x, mem, positions, pre_g, post_g, mem_g, w_mem, a_w_in, lb_logits, out_g, a_w_out, kv_g,
          w_kv, b_w_in, sinks, b_w_out, c_ident, c_level, c_window, c_freq, h_dram, k_dram, m_dram, out):
    ctx = ExitStack()
    with ctx:
        def sem(name):
            return ctx.enter_context(nc.semaphore(name))

        def psum(name, shape, dt=F32):
            return ctx.enter_context(nc.psum_tensor(name, shape, dt))

        place = [-(-nc.sbuf_base // 64) * 64]

        def sb(name, shape, dt=F32, at=None):
            size = int(np.prod(shape[1:])) * (1 if dt == U8 else 4)
            if at is None:
                at = place[0]
                place[0] += -(-size // 64) * 64
            return nc.alloc_sbuf_tensor_at(name, shape, dt, offset=at)

        X = sb("X", [P, 16, T], F32R)
        O = sb("O", [P, EB, T])
        w_raw = sb("w_raw", [P, 2, EB, P])
        w_hi = sb("w_hi", [P, 2, EB, P], F32R)
        w_lo = sb("w_lo", [P, 2, EB, P], F32R)
        ident = sb("ident", [P, P])
        ones = sb("ones", [P, P])
        r2_at = place[0]
        level_mask = sb("level_mask", [P, LEVELS, HALF], U8)
        ST = sb("ST", [P, 2, P])
        R2 = sb("R2", [P, T], at=r2_at)
        assert r2_at + 4 * T <= place[0]
        window = sb("window", [P, 2 * P])
        pre_col = sb("pre_col", [P, 2, KB])
        post_col = sb("post_col", [P, 2, KB])
        mem_col = sb("mem_col", [P, 2, KB])
        kv_col = sb("kv_col", [P, KB])
        out_col = sb("out_col", [P, HEADS])
        lb2 = sb("lb2", [P, 2, HEADS])
        lb = sb("lb", [P, HEADS])
        oml = sb("oml", [P, HEADS])
        lbt = sb("lbt", [P, 2, HEADS])
        freq = sb("freq", [P, 1])
        sink_b = sb("sink_b", [P, 4 * GROUPS])
        eps_c = sb("eps_c", [P, 1])
        EL = sb("EL", [P, CH])
        pad = sb("pad", [P, 1])
        sm_max = sb("sm_max", [P, 2, 4])
        sm_neg = sb("sm_neg", [P, 2, 4])
        sm_den = sb("sm_den", [P, 2, 4])
        sm_inv = sb("sm_inv", [P, 2, 4])
        sm_snk = sb("sm_snk", [P, 2, 4])

        arena = place[0]
        ROW = 4 * T

        def ar(name, row, shape, dt=F32):
            return sb(name, shape, dt, at=arena + int(row * ROW))

        CUM = ar("CUM", 0, [P, T])
        KK = ar("KK", 1, [P, T])
        Q = ar("Q", 2, [P, 2, T])
        E2 = ar("E2", 4, [P, 2, T])
        KH = ar("KH", 6, [P, 2, T])
        QH = ar("QH", 8, [P, 2, HALF])
        PT = ar("PT", 9, [P, T])
        TV = ar("TV", 10, [P, T])
        SQ = ar("SQ", 11, [P, HALF])
        RN = ar("RN", 11.5, [P, HALF])
        RB0 = PT
        MHI = ar("MHI", 0, [P, KB, MT], F32R)
        MLO = ar("MLO", 2, [P, KB, MT], F32R)
        MP = ar("MP", 4, [P, 2, 2, MT])
        PTM = ar("PTM", 5, [P, 2, T])
        MS = [ar("MS0", 5, [P, KB, MT]), ar("MS1", 4, [P, KB, MT])]
        MSQ = ar("MSQ", 8, [P, 2, MT])
        MQ = ar("MQ", 7, [P, T])
        MT1 = ar("MT1", 8, [P, T])
        KM = ar("KM", 9, [P, MT])
        TVM = ar("TVM", 9.25, [P, MT])
        VM = ar("VM", 9.5, [P, 2, P])
        RBM = MSQ[:, 0, :]
        ROPE_AT = 10
        rope_c = ar("rope_c", ROPE_AT, [P, T])
        rope_s = ar("rope_s", ROPE_AT + 1, [P, T])
        assert arena + (ROPE_AT + 2) * ROW <= nc.sbuf_usable_end, (arena, nc.sbuf_usable_end)
        OLO = ar("OLO", 0, [P, 8, T], F32R)
        HR = ar("HR", 0, [P, KB, T])
        RB = ar("RB", 8, [P, T])
        KST = ar("KST", 0, [P, 2, T])
        KP = ar("KP", 2, [P, 2, T])
        VALL = ar("VALL", 4, [P, CH, 2 * P])
        VG = ar("VG", 6, [P, CH, DH])
        QR = ar("QR", 6.5, [P, 2, T])
        PTS = ar("PTS", 8.5, [P, 2, 4, P])
        LMF = O[:, 8:12, :].rearrange("p a t -> p (a t)")[:, 0:LEVELS * HALF].rearrange("p (l t) -> p l t", l=LEVELS)
        T1 = O[:, 8, :]
        T2 = O[:, 9, :]
        VN = O[:, 10, :]
        KDT = O[:, 11, :]
        RA = O[:, 9, :]
        RTI = ar("RTI", 9, [P, T], I32)
        RTK = ar("RTK", 9, [P, T])
        SM = [O[:, 10, :], O[:, 11, :], ar("SM2", 0, [P, T])]

        Z = psum("Z", [P, 2, T])
        SC = psum("SC", [P, 2, HALF])
        OB = psum("OB", [P, HALF])
        MB = psum("MB", [P, HALF])

        SCF = SC[:, :, :].rearrange("p a t -> p (a t)")

        s_const = sem("s_const")
        s_x_in = [sem(f"s_x_in{e}") for e in range(KB)]
        s_memset = sem("s_memset")
        s_w_in = [sem("s_w_in0"), sem("s_w_in1")]
        s_w_scaled = sem("s_w_scaled")
        s_whi = sem("s_whi")
        s_wlo = sem("s_wlo")
        s_whi_x = sem("s_whi_x")
        s_wlo_x = sem("s_wlo_x")
        s_mm = sem("s_mm")
        s_lb = sem("s_lb")
        s_level_in = sem("s_level_in")
        s_level = sem("s_level")
        s_lbd = sem("s_lbd")
        s_xsq = sem("s_xsq")
        s_xadd = sem("s_xadd")
        s_xss = sem("s_xss")
        s_rb0 = sem("s_rb0")
        s_xs = sem("s_xs")
        s_xp = sem("s_xp")
        s_xhi = sem("s_xhi")
        s_xlo = sem("s_xlo")
        s_h_out = [sem("s_h_out0"), sem("s_h_out1")]
        s_sg = sem("s_sg")
        s_clamp = sem("s_clamp")
        s_silu = sem("s_silu")
        s_k = sem("s_k")
        s_cum = sem("s_cum")
        s_tv = sem("s_tv")
        s_vT = sem("s_vT")
        s_vn = sem("s_vn")
        s_dif = sem("s_dif")
        s_dec = sem("s_dec")
        s_hat = sem("s_hat")
        s_qc = sem("s_qc")
        s_kd = sem("s_kd")
        s_el = sem("s_el")
        s_diag = sem("s_diag")
        s_diag_ev = sem("s_diag_ev")
        s_lev = sem("s_lev")
        s_pred = sem("s_pred")
        s_kdT = sem("s_kdT")
        s_kdt = sem("s_kdt")
        s_stm = sem("s_stm")
        s_st = sem("s_st")
        s_fin = sem("s_fin")
        s_osq = sem("s_osq")
        s_og = sem("s_og")
        s_oss = sem("s_oss")
        s_rnl = sem("s_rnl")
        s_rn = sem("s_rn")
        s_on = sem("s_on")
        s_mem_in = sem("s_mem_in")
        s_mem_out = sem("s_mem_out")
        s_msq = sem("s_msq")
        s_mss = sem("s_mss")
        s_rbm = sem("s_rbm")
        s_mx = sem("s_mx")
        s_mhi = sem("s_mhi")
        s_mlo = sem("s_mlo")
        s_msg = sem("s_msg")
        s_mclamp = sem("s_mclamp")
        s_mgate = sem("s_mgate")
        s_mq = sem("s_mq")
        s_km = sem("s_km")
        s_tvm = sem("s_tvm")
        s_vmT = sem("s_vmT")
        s_vm = sem("s_vm")
        s_msc = sem("s_msc")
        s_mmax = sem("s_mmax")
        s_mneg = sem("s_mneg")
        s_mexp = sem("s_mexp")
        s_minv = sem("s_minv")
        s_mpn = sem("s_mpn")
        s_mpT = sem("s_mpT")
        s_mpt = sem("s_mpt")
        s_mpv = sem("s_mpv")
        s_mo = sem("s_mo")
        s_pos = sem("s_pos")
        s_rt = sem("s_rt")
        s_rtg = sem("s_rtg")
        s_rope = sem("s_rope")
        s_ohi = sem("s_ohi")
        s_olo = sem("s_olo")
        s_ysq = sem("s_ysq")
        s_y = sem("s_y")
        s_acc = sem("s_acc")
        s_yss = sem("s_yss")
        s_rbl = sem("s_rbl")
        s_rb = sem("s_rb")
        s_hr = [sem(f"s_hr{j}") for j in range(KB)]
        s_yp = sem("s_yp")
        s_hp = sem("s_hp")
        s_yn = sem("s_yn")
        s_h = sem("s_h")
        s_hsq = sem("s_hsq")
        s_hss = sem("s_hss")
        s_rb2l = sem("s_rb2l")
        s_rb2 = sem("s_rb2")
        s_zs = sem("s_zs")
        s_mz = sem("s_mz")
        s_out = [sem("s_out0"), sem("s_out1")]
        s_ra = sem("s_ra")
        s_rot = sem("s_rot")
        s_k_out = sem("s_k_out")
        s_tvs = sem("s_tvs")
        s_vsT = sem("s_vsT")
        s_vs = sem("s_vs")
        s_kp = sem("s_kp")
        s_kz = sem("s_kz")
        s_vg = sem("s_vg")
        s_ssg = sem("s_ssg")
        s_sclamp = sem("s_sclamp")
        s_sgate = sem("s_sgate")
        s_sc = sem("s_sc")
        s_msk = sem("s_msk")
        s_smax = sem("s_smax")
        s_sm = sem("s_sm")
        s_sneg = sem("s_sneg")
        s_sexp = sem("s_sexp")
        s_sden = sem("s_sden")
        s_sinv = sem("s_sinv")
        s_spn = sem("s_spn")
        s_spT = sem("s_spT")
        s_spt = sem("s_spt")
        s_spv = sem("s_spv")
        s_so = sem("s_so")

        def bc(ap, n):
            return ap.unsqueeze(1).to_broadcast([P, n, ap.shape[-1]])

        DVE_ROWS = ((0, 2, 4, 6), (0, 1, 3, 4, 6))
        POOL_ROWS = ((1, 3, 5, 7), (2, 5, 7))

        def wait_row(eng, layer, j):
            for semaphore, rows in ((s_h, DVE_ROWS), (s_hp, POOL_ROWS)):
                if j in rows[layer]:
                    eng.wait_ge(semaphore, layer * len(rows[0]) + rows[layer].index(j) + 1)

        def low_row(e):
            return X[:, 12 + e, :] if e < 4 else OLO[:, (0, 1, 2, 3, 7, 4, 5, 6)[e - 4], :]

        block = ctx.enter_context(nc.Block())
        N_CONST = 10

        @block.sync
        def _(sp):
            for e in range(KB):
                sp.dma_start(O[:, e, :], x[:, e, :]).then_inc(s_x_in[e], 16)
            for dst, src in (
                (ident[:, :], c_ident), (window[:, :], c_window), (freq[:, :], c_freq),
                (pre_col[:, :, :], pre_g), (post_col[:, :, :], post_g), (mem_col[:, :, :], mem_g), (kv_col[:, :], kv_g),
                (out_col[:, :], out_g), (lb2[:, :, :], lb_logits),
                (sink_b[:, :], sinks[0:1, :].to_broadcast([P, 4 * GROUPS])),
            ):
                sp.dma_start(dst, src).then_inc(s_const, 16)

            def load(t, src, rows=KB):
                wait(sp, s_wlo, t.n - 1)
                sp.dma_start(w_raw[:, t.slot, 0:rows, :], src).then_inc(s_w_in[t.slot], 16)

            def part(w, at):
                return w[bass.ds(at, 1)].rearrange("a p k c -> (a p) k c")

            def load_head(h):
                for i, which in enumerate((0, 3, 1, 2)):
                    load(Tile(N_H, h, i), part(a_w_in, which * KB + h))
                    if isinstance(h, int) and i == 0:
                        sp.dma_start(LMF, c_level).then_inc(s_level_in, 16)

            load_head(0)
            with sp.Fori(1, HEADS) as h:
                load_head(h)

            def load_mem(base, layer, m):
                w, at = (a_w_in, 4 * KB) if layer == 0 else (b_w_in, 2 * KB)
                load(Tile(base, m, 0), part(w, at + MH + m))
                load(Tile(base, m, 1), part(w, at + m))
                load(Tile(base, m, 2), part(w_mem, layer * 2 * MH + m))
                load(Tile(base, m, 3), part(w_mem, layer * 2 * MH + MH + m))

            def load_mem_phase(base, layer):
                load_mem(base, layer, 0)
                if layer == 0:
                    sp.wait_ge(s_lev, LEVELS * HEADS)
                    sp.wait_ge(s_qc, HEADS)
                    sp.dma_start(MS[0][:, :, :], mem).then_inc(s_mem_in, 16)
                    sp.wait_ge(s_mx, KB // 2)
                    sp.dma_start(m_dram, MS[0][:, :, :]).then_inc(s_mem_out, 16)
                else:
                    sp.wait_ge(s_vg, GROUPS)
                    sp.wait_ge(s_mem_out, 16)
                    sp.dma_start(MS[1][:, :, :], m_dram).then_inc(s_mem_in, 16)
                with sp.Fori(1, MH) as m:
                    load_mem(base, layer, m)

            def load_out(base, layer):
                with sp.Fori(0, KB // 4) as s:
                    for i in range(4):
                        if i == 2:
                            sp.wait_ge(s_wlo_x, layer + 1)
                        load(Tile(base, s, i), part(a_w_out if layer == 0 else b_w_out, 4 * s + i), EB)

            load_mem_phase(N_AM, 0)
            load_out(N_AO, 0)
            for i in range(2):
                load(Tile(N_K, 0, i), part(w_kv, i))

            def residual(layer, src, dst, stored):
                sp.wait_ge(s_mm, (N_BO if layer else N_AO) + KB)
                for j in range(KB):
                    sp.dma_start(HR[:, j, :], src[:, j, :]).then_inc(s_hr[j], 16)
                for j in range(KB):
                    wait_row(sp, layer, j)
                    sp.dma_start(dst[:, j, :], O[:, j, :]).then_inc(stored[j % 2], 16)

            residual(0, x, h_dram, s_h_out)
            for i in range(2, 4):
                load(Tile(N_K, 0, i), part(w_kv, i))
            with sp.Fori(0, GROUPS) as g:
                for i in range(4):
                    at = g * 2 + i % 2
                    load(Tile(N_S, g, i), part(b_w_in, at + KB if i < 2 else at))
            load_mem_phase(N_BM, 1)
            load_out(N_BO, 1)
            for stored in s_h_out:
                sp.wait_ge(stored, 16 * KB // 2)
            residual(1, h_dram, out, s_out)
            for stored in s_out:
                sp.wait_ge(stored, 16 * KB // 2)

        @block.tensor
        def _(pe):
            def x_hi(e, half):
                return X[:, e, half * HALF:(half + 1) * HALF]

            def x_lo(e, half):
                return X[:, 8 + e, half * HALF:(half + 1) * HALF]

            def o_lo(e, half):
                return low_row(e)[:, half * HALF:(half + 1) * HALF]

            def tile(t, between=None, rows=KB, hi=x_hi, lo=x_lo, ready=None):
                wait(pe, s_wlo, t.n + 1)
                for e in range(rows):
                    if ready:
                        ready(e)
                    wh, wl = w_hi[:, t.slot, e, :], w_lo[:, t.slot, e, :]
                    for a, (w, act) in enumerate(((wh, hi), (wh, lo), (wl, hi))):
                        for half in range(2):
                            mm = nc.tensor.matmul(Z[:, t.slot, half * HALF:(half + 1) * HALF], w, act(e, half),
                                                  start=(e == 0 and a == 0), stop=(e == rows - 1 and a == 2))
                    if e == rows - 1:
                        mm.then_inc(s_mm, 1)
                    for u in (between or {}).get(e, ()):
                        u()

            def mem_tile(t, between=()):
                wait(pe, s_wlo, t.n + 1)
                for e in range(KB):
                    for a, (w, act) in enumerate(((w_hi, MHI), (w_hi, MLO), (w_lo, MHI))):
                        mm = nc.tensor.matmul(Z[:, t.slot, 0:MT], w[:, t.slot, e, :], act[:, e, :],
                                              start=(e == 0 and a == 0), stop=(e == KB - 1 and a == 2))
                mm.then_inc(s_mm, 1)
                for u in between:
                    u()

            pe.wait_ge(s_memset, 1)
            for i in range(KB // 2):
                pe.wait_ge(s_xadd, i + 1)
                for half in range(2):
                    mm = nc.tensor.matmul(SC[:, half, :], ones[:, :], E2[:, i % 2, half * HALF:(half + 1) * HALF],
                                          start=(i == 0), stop=(i == KB // 2 - 1))
                mm.then_inc(s_xss, 1)
            pe.wait_ge(s_const, 16 * N_CONST)

            def hgrn_units(r):
                def v_turn(part):
                    def unit():
                        if part == 0:
                            pe.wait_ge(s_tv, r + 1)
                        else:
                            pe.wait_ge(s_vn, 2 * r + 1)
                        for c in range(4):
                            at = (4 * part + c) * P
                            mm = nc.tensor.transpose(MB[:, c * P:(c + 1) * P], TV[:, at:at + P], ident[:, :])
                        mm.then_inc(s_vT, 1)
                    return unit

                def diagonal(part):
                    def unit():
                        pe.wait_ge(s_k, r + 1)
                        pe.wait_ge(s_silu, 2 * r + 1)
                        if part == 1:
                            pe.wait_ge(s_rnl, 2 * r + 1)
                        for c in range(4):
                            at = (4 * part + c) * P
                            mm = nc.tensor.matmul(SC[:, part, c * P:(c + 1) * P], KK[:, at:at + P],
                                                  q_of(r)[:, at:at + P], start=True, stop=True)
                        mm.then_inc(s_diag, 1)
                    return unit

                def level(l):
                    def unit():
                        pe.wait_ge(s_hat, LEVELS * r + l + 1)
                        if l < 2:
                            pe.wait_ge(s_diag_ev, 2 * r + l + 1)
                        else:
                            pe.wait_ge(s_pred, LEVELS * r + l - 1)
                        for c in range(CH):
                            mm = nc.tensor.matmul(SC[:, l % 2, c * 64:(c + 1) * 64], KH[:, l % 2, c * P:(c + 1) * P],
                                                  QH[:, l % 2, c * 64:(c + 1) * 64], start=True, stop=True)
                        mm.then_inc(s_lev, 1)
                    return unit

                def kd_turn(part):
                    def unit():
                        if part == 0:
                            pe.wait_ge(s_kd, r + 1)
                            pe.wait_ge(s_vn, 2 * r + 2)
                        else:
                            pe.wait_ge(s_kdt, 2 * r + 1)
                        for c in range(4):
                            at = (4 * part + c) * P
                            mm = nc.tensor.transpose(MB[:, c * P:(c + 1) * P], E2[:, 0, at:at + P], ident[:, :])
                        mm.then_inc(s_kdT, 1)
                    return unit

                def chunk(c):
                    def unit():
                        o = OB[:, (c % 4) * P:(c % 4 + 1) * P]
                        if c == 0:
                            pe.wait_ge(s_pred, LEVELS * (r + 1))
                            pe.wait_ge(s_kdt, 2 * r + 2)
                            pe.wait_ge(s_qc, r + 1)
                        if c == 4:
                            pe.wait_ge(s_osq, 2 * r + 1)
                            pe.wait_ge(s_og, 2 * r + 1)
                        mm = nc.tensor.matmul(o, VN[:, c * P:(c + 1) * P], PT[:, c * P:(c + 1) * P],
                                              start=True, stop=(c == 0))
                        if c > 0:
                            pe.wait_ge(s_st, (CH - 1) * r + c)
                            mm = nc.tensor.matmul(o, ST[:, c % 2, :], q_of(r)[:, c * P:(c + 1) * P],
                                                  start=False, stop=True)
                        if c % 4 == 3:
                            mm.then_inc(s_fin, 1)
                        if c < CH - 1:
                            nc.tensor.matmul(MB[:, 0:P], KDT[:, c * P:(c + 1) * P], VN[:, c * P:(c + 1) * P],
                                             start=True, stop=True).then_inc(s_stm, 1)
                    return unit

                def norm(part):
                    def unit():
                        pe.wait_ge(s_osq, 2 * r + part + 1)
                        nc.tensor.matmul(SC[:, part, :], ones[:, :], SQ[:, :], start=True, stop=True).then_inc(s_oss, 1)
                    return unit

                v, d, l, kd, c, n = v_turn, diagonal, level, kd_turn, chunk, norm
                return (
                    {0: [d(0)], 1: [d(1)], 2: [v(0)], 3: [l(0)], 4: [v(1)], 5: [l(1)], 7: [l(2)]},
                    {0: [l(3)], 2: [l(4)], 4: [l(5)], 6: [l(6)]},
                    {1: [kd(0)], 2: [kd(1)], 3: [c(0)], 4: [c(1)], 5: [c(2)], 6: [c(3)]},
                    {0: [c(4)], 1: [n(0)], 2: [c(5)], 3: [c(6)], 5: [c(7)], 7: [n(1)]},
                )

            def q_of(r):
                return Q[:, r % 2, :] if isinstance(r, int) else Q[:, bass.ds(r % 2, 1), :].rearrange("p a t -> p (a t)")

            def head_stage(h, units):
                tq, tg, tf, tv = (Tile(N_H, h, i) for i in range(4))
                first = isinstance(h, int) and h == 0
                if not first:
                    pe.wait_ge(s_sg, 10 * h - 3)
                tile(tq, units[0], ready=(lambda e: pe.wait_ge(s_xlo, e + 1)) if first else None)
                if not first:
                    pe.wait_ge(s_tv, h)
                tile(tg, units[1])
                pe.wait_ge(s_silu, 2 * h + 1)
                tile(tf, units[2])
                pe.wait_ge(s_silu, 2 * h + 2)
                tile(tv, units[3])

            def alone(steps):
                for step in steps:
                    for e in sorted(step):
                        for u in step[e]:
                            u()

            head_stage(0, (None,) * 4)
            with pe.Fori(1, HEADS) as h:
                head_stage(h, hgrn_units(h - 1))

            def mem_sum(e):
                def unit():
                    if e == 0:
                        pe.wait_ge(s_mgate, 1)
                    pe.wait_ge(s_msq, e + 1)
                    nc.tensor.matmul(Z[:, 0, HALF:HALF + MT], ones[:, :], MSQ[:, e % 2, :], start=(e == 0),
                                     stop=(e == KB - 1)).then_inc(s_mss, 1)
                return unit

            u = hgrn_units(HEADS - 1)
            pe.wait_ge(s_sg, 10 * HEADS)
            tile(Tile(N_AM, 0, 0), u[0])
            pe.wait_ge(s_tv, HEADS)
            tile(Tile(N_AM, 0, 1), u[1])
            for e, after in enumerate((2, 2, 3, 3, 4, 4, 5, 5)):
                u[2][after].append(mem_sum(e))
            alone(u[2:])

            def mem_units(layer, m, last=False):
                r = MH * layer + m

                def v_turn():
                    pe.wait_ge(s_tvm, r + 1)
                    for a in range(2):
                        mm = nc.tensor.transpose(MB[:, a * P:(a + 1) * P], TVM[:, a * P:(a + 1) * P], ident[:, :])
                    mm.then_inc(s_vmT, 1)

                def scores(j):
                    def unit():
                        if j == 0:
                            pe.wait_ge(s_km, r + 1)
                            pe.wait_ge(s_mq, r + 1)
                        if j >= 2:
                            pe.wait_ge(s_mexp, 4 * r + j - 1)
                        for a in range(2):
                            at = (2 * j + a) * P
                            mm = nc.tensor.matmul(SC[:, j % 2, a * MT:(a + 1) * MT], MQ[:, at:at + P], KM[:, :],
                                                  start=True, stop=True)
                        mm.then_inc(s_msc, 1)
                    return unit

                def turn(j):
                    def unit():
                        pe.wait_ge(s_mpn, 4 * r + j + 1)
                        if j == 0:
                            pe.wait_ge(s_vm, r + 1)
                        else:
                            pe.wait_ge(s_mpt, 4 * r + j)
                        for b in range(2):
                            for a in range(2):
                                mm = nc.tensor.transpose(MB[:, (2 * b + a) * P:(2 * b + a + 1) * P],
                                                         MP[:, j % 2, a, b * P:(b + 1) * P], ident[:, :])
                        mm.then_inc(s_mpT, 1)
                    return unit

                def values(half):
                    def unit():
                        pe.wait_ge(s_mpt, 4 * r + 2 * half + 2)
                        if half == 1:
                            pe.wait_ge(s_mo, 2 * r + 1)
                        for b in range(2):
                            mm = nc.tensor.matmul(OB[:, :], VM[:, b, :], PTM[:, b, half * HALF:(half + 1) * HALF],
                                                  start=(b == 0), stop=(b == 1))
                        mm.then_inc(s_mpv, 1)
                    return unit

                s, t, v = scores, turn, values
                if last:
                    return ([v_turn, s(0), s(1)],
                            {1: [t(0)], 2: [s(2), t(1)], 3: [s(3)], 4: [t(2)], 5: [v(0)], 6: [t(3)], 7: [v(1)]})
                return ({0: [v_turn], 1: [s(0)], 2: [s(1)], 4: [t(0)], 5: [s(2)], 6: [t(1)], 7: [s(3)]},
                        {0: [t(2)], 1: [t(3)], 3: [v(0)], 5: [v(1)]})

            def mem_stage(base, layer, m, units):
                r = MH * layer + m
                tg, tq, tk, tv = (Tile(base, m, i) for i in range(4))
                if units:
                    pe.wait_ge(s_km, r)
                    tile(tg, units[0])
                    pe.wait_ge(s_tvm, r)
                    tile(tq, units[1])
                else:
                    pe.wait_ge(s_mlo, 4 * (layer + 1))
                pe.wait_ge(s_mgate, r + 1)
                mem_tile(tk)
                pe.wait_ge(s_mq, r + 1)
                mem_tile(tv)

            def mem_phase(base, layer):
                mem_stage(base, layer, 0, None)
                with pe.Fori(1, MH) as m:
                    mem_stage(base, layer, m, mem_units(layer, m - 1))

            def out_phase(base, layer):
                def one(s, i, ready=None, between=None):
                    t = Tile(base, s, i)
                    if not (isinstance(s, int) and s == 0 and i < 2):
                        pe.wait_ge(s_y, KB * layer + 4 * s + i - 1)
                    tile(t, between, rows=EB, lo=o_lo, ready=ready)

                def split(e):
                    pe.wait_ge(s_olo, EB * layer + e + 1)

                r = MH * (layer + 1)
                before, between = mem_units(layer, MH - 1, last=True)
                for u in before:
                    u()
                pe.wait_ge(s_wlo_x, layer + 1)
                one(0, 0, split, between)
                for i in range(1, 4):
                    one(0, i)
                with pe.Fori(1, KB // 4) as s:
                    for i in range(4):
                        one(s, i)
                pe.wait_ge(s_acc, (KB - 1) * (layer + 1))
                for half in range(2):
                    nc.tensor.matmul(SC[:, half, :], ones[:, :], O[:, 10, half * HALF:(half + 1) * HALF],
                                     start=True, stop=False)
                pe.wait_ge(s_ysq, KB * (layer + 1))
                for half in range(2):
                    mm = nc.tensor.matmul(SC[:, half, :], ones[:, :], O[:, 9, half * HALF:(half + 1) * HALF],
                                          start=False, stop=True)
                mm.then_inc(s_yss, 1)

            mem_phase(N_AM, 0)
            out_phase(N_AO, 0)

            def row_ready(j):
                pe.wait_ge(s_hsq, j + 1)
                if j == 0:
                    pe.wait_ge(s_rb, 1)
                for half in range(2):
                    mm = nc.tensor.matmul(SC[:, half, :], ones[:, :], O[:, 8 + j % 2, half * HALF:(half + 1) * HALF],
                                          start=(j == 0), stop=(j == KB - 1))
                mm.then_inc(s_hss, 1)
                pe.wait_ge(s_xlo, KB + j + 1)

            pe.wait_ge(s_y, KB)
            tile(Tile(N_K, 0, 0), ready=row_ready)
            tile(Tile(N_K, 0, 1))
            pe.wait_ge(s_rot, 1)
            tile(Tile(N_K, 0, 2))
            pe.wait_ge(s_rot, 2)
            tile(Tile(N_K, 0, 3))
            for i in range(2):
                pe.wait_ge(s_tvs, i + 1)
                for part in range(2):
                    if i or part:
                        pe.wait_ge(s_vs, 2 * i + part)
                    for c in range(4):
                        at = (4 * part + c) * P
                        mm = nc.tensor.transpose(MB[:, c * P:(c + 1) * P], T1[:, at:at + P] if i == 0 else RA[:, at:at + P],
                                                 ident[:, :])
                    mm.then_inc(s_vsT, 1)

            def swa_units(r, begin=SWA_ROUNDS):
                def scores(b):
                    def unit():
                        if b == 0:
                            pe.wait_ge(s_kp, 16 * 4 * (r + 1))
                            pe.wait_ge(s_rot, 2 + 2 * r + 2)
                        for p in range(2):
                            if b:
                                pe.wait_ge(s_msk, 16 * r + 2 * b + p - 1)
                            lo = P if b == 0 else 0
                            sc = SC[:, p, :].rearrange("q (h k) -> q h k", h=2)
                            mm = nc.tensor.matmul(sc[:, :, lo:2 * P], QR[:, p, b * P:(b + 1) * P],
                                                  KP[:, :, (b - 1) * P + lo:(b + 1) * P], start=True, stop=True)
                            mm.then_inc(s_sc, 1)
                    return unit

                def turn(b, k):
                    def unit():
                        pe.wait_ge(s_spn, CH * r + b + 1)
                        if b:
                            pe.wait_ge(s_spt, 15 * r + 2 * b - 1 + k)
                        for h in range(4):
                            mm = nc.tensor.transpose(MB[:, h * P:(h + 1) * P],
                                                     SM[b % 3][:, (2 * h + k) * P:(2 * h + k + 1) * P], ident[:, :])
                        mm.then_inc(s_spT, 1)
                    return unit

                def values(b):
                    def unit():
                        pe.wait_ge(s_spt, 15 * r + 2 * b + 1)
                        if b == 0:
                            pe.wait_ge(s_vg, r + 1)
                        else:
                            pe.wait_ge(s_so, CH * r + b)
                        blocks = (1,) if b == 0 else (0, 1)
                        for odd in range(2):
                            for k in blocks:
                                heads = PTS[:, k, odd:4:2, :]
                                mm = nc.tensor.matmul(OB[odd * DH:(odd + 1) * DH, 0:2 * P],
                                                      VG[:, b - 1 + k, :], heads, start=(k == blocks[0]), stop=(k == 1))
                        mm.then_inc(s_spv, 1)
                    return unit

                steps = [{}, {}, {}, {}]

                def put(k, unit):
                    steps[k // KB].setdefault(k % KB, []).append(unit)

                for i, k in enumerate(begin):
                    b = i - 2
                    if i < CH:
                        put(k, scores(i))
                    if b > 0:
                        put(k, turn(b, 0))
                    if b >= 0:
                        put(k + 1, turn(b, 1))
                    if b >= 0:
                        put(min(k + 2, 4 * KB - 1), values(b))
                return steps

            def swa_stage(g, units):
                tiles = [Tile(N_S, g, i) for i in range(4)]
                pe.wait_ge(s_rot, 2 + 2 * g - 1) if not (isinstance(g, int) and g == 0) else pe.wait_ge(s_tvs, 1)
                tile(tiles[0], units[0])
                pe.wait_ge(s_rot, 2 + 2 * g) if not (isinstance(g, int) and g == 0) else pe.wait_ge(s_tvs, 2)
                tile(tiles[1], units[1])
                pe.wait_ge(s_sgate, 2 * g + 1)
                tile(tiles[2], units[2])
                pe.wait_ge(s_sgate, 2 * g + 2)
                tile(tiles[3], units[3])

            swa_stage(0, (None,) * 4)
            with pe.Fori(1, GROUPS) as g:
                swa_stage(g, swa_units(g - 1))
            u = swa_units(GROUPS - 1, SWA_LAST_ROUNDS)
            pe.wait_ge(s_rot, 2 + 2 * GROUPS - 1)
            tile(Tile(N_BM, 0, 0), u[0])
            pe.wait_ge(s_rot, 2 + 2 * GROUPS)
            tile(Tile(N_BM, 0, 1), u[1])
            alone(u[2:])

            mem_phase(N_BM, 1)
            out_phase(N_BO, 1)
        @block.scalar
        def _(act):
            A = nc.scalar.activation

            def w_high(t, scaled=None, rows=slice(0, KB), extra=False):
                act.wait_ge(s_w_in[t.slot], 16 * (t.before + 1))
                if scaled is not None:
                    act.wait_ge(s_w_scaled, scaled)
                wait(act, s_mm, t.n - 1)
                A(w_hi[:, t.slot, rows, :], w_raw[:, t.slot, rows, :], ACT.Copy).then_inc(s_whi_x if extra else s_whi, 1)

            def sigmoid(z, tmp, steps, at, clamped, clamp_at):
                A(tmp, z, ACT.Exp, scale=-1.0).then_inc(steps, 1)
                act.wait_ge(clamped, clamp_at)
                A(tmp, tmp, ACT.Ln, bias=1.0).then_inc(steps, 1)
                act.wait_ge(steps, at + 2)
                A(tmp, tmp, ACT.Exp, scale=-1.0).then_inc(steps, 1)

            nc.scalar.preload_act_table_set("natural_log_exp_and_others")
            for e in range(KB):
                act.wait_ge(s_x_in[e], 16)
                if e >= 2:
                    act.wait_ge(s_xadd, e // 2)
                A(KH[:, e % 2, :], O[:, e, :], ACT.Square).then_inc(s_xsq, 1)
            w_high(Tile(N_H, 0, 0))
            act.wait_ge(s_xss, KB // 2)
            act.wait_ge(s_memset, 2)
            A(RB0[:, :], SCF, ACT.Ln, scale=1.0 / D, bias=eps_c[:, :]).then_inc(s_rnl, 1)
            act.wait_ge(s_rnl, 1)
            A(RB0[:, :], RB0[:, :], ACT.Exp, scale=-0.5).then_inc(s_rb0, 1)
            for e in range(KB):
                act.wait_ge(s_xp if e % 2 else s_xs, e // 2 + 1)
                A(X[:, e, :], O[:, e, :], ACT.Copy, scale=pre_col[:, 0, e:e + 1]).then_inc(s_xhi, 1)
            act.wait_ge(s_lbd, 1)
            A(lbt[:, :, :], lb2[:, :, :], ACT.Exp).then_inc(s_lb, 1)

            def hgrn_steps(r):
                def v_out():
                    act.wait_ge(s_mm, 4 * r + 4)
                    A(TV[:, :], Z[:, 1, :], ACT.Copy).then_inc(s_tv, 1)

                def v_copy(part):
                    act.wait_ge(s_vT, 2 * r + part + 1)
                    A(VN[:, part * HALF:(part + 1) * HALF], MB[:, :], ACT.Copy).then_inc(s_vn, 1)

                def level(l):
                    half = 1 << l
                    e = E2[:, l % 2, :].rearrange("p (n f i) -> p n f i", f=2, i=half)
                    act.wait_ge(s_dif, 8 * r + l + 1)
                    A(e[:, :, 0, :], e[:, :, 0, :], ACT.Exp, scale=-1.0)
                    A(e[:, :, 1, :], e[:, :, 1, :], ACT.Exp).then_inc(s_dec, 1)

                def q_decay():
                    act.wait_ge(s_hat, LEVELS * r + 6)
                    A(E2[:, 1, :], CUM[:, :], ACT.Exp).then_inc(s_dec, 1)
                    A(EL[:, :], CUM[:, P - 1:T:P], ACT.Exp).then_inc(s_el, 1)

                def k_decay():
                    act.wait_ge(s_dif, 8 * r + 8)
                    A(E2[:, 0, :], E2[:, 0, :], ACT.Exp).then_inc(s_dec, 1)

                def kd_copy(part):
                    act.wait_ge(s_kdT, 2 * r + part + 1)
                    A(KDT[:, part * HALF:(part + 1) * HALF], MB[:, :], ACT.Copy).then_inc(s_kdt, 1)

                def square(part):
                    act.wait_ge(s_fin, 2 * r + part + 1)
                    if part:
                        act.wait_ge(s_oss, 2 * r + 1)
                    A(SQ[:, :], OB[:, :], ACT.Square).then_inc(s_osq, 1)

                def inverse(part):
                    act.wait_ge(s_oss, 2 * r + part + 1)
                    if part:
                        act.wait_ge(s_on, 2 * r + 1)
                    A(RN[:, :], SC[:, part, :], ACT.Ln, scale=1.0 / P, bias=eps_c[:, :]).then_inc(s_rnl, 1)
                    act.wait_ge(s_rnl, 2 * r + part + 2)
                    A(RN[:, :], RN[:, :], ACT.Exp, scale=-0.5).then_inc(s_rn, 1)

                return v_out, v_copy, level, q_decay, k_decay, kd_copy, square, inverse

            def mem_squares():
                act.wait_ge(s_mem_in, 16)
                for e in range(KB):
                    if e >= 2:
                        act.wait_ge(s_mss, e - 1)
                    A(MSQ[:, e % 2, :], MS[0][:, e, :], ACT.Square).then_inc(s_msq, 1)

            def mem_inverse():
                act.wait_ge(s_mss, KB)
                A(RBM, Z[:, 0, HALF:HALF + MT], ACT.Ln, scale=1.0 / D, bias=eps_c[:, :]).then_inc(s_rbm, 1)
                act.wait_ge(s_rbm, 1)
                A(RBM, RBM, ACT.Exp, scale=-0.5).then_inc(s_rbm, 1)

            def mem_high(layer, first, end):
                for e in range(first, end):
                    if layer == 0:
                        act.wait_ge(s_mx, e // 2 + 1)
                    elif e == 0:
                        act.wait_ge(s_mem_in, 32)
                    A(MHI[:, e, :], MS[layer][:, e, :], ACT.Copy, scale=mem_col[:, layer, e:e + 1]).then_inc(s_mhi, 1)

            def gate_step(layer, step):
                r = MH * layer
                if step == 0:
                    if layer:
                        act.wait_ge(s_mz, 1)
                        act.wait_ge(s_sgate, 2 * GROUPS)
                    else:
                        act.wait_ge(s_mm, N_AM + 1)
                    A(T1, Z[:, 0, :], ACT.Exp, scale=-1.0).then_inc(s_msg, 1)
                elif step == 1:
                    act.wait_ge(s_mclamp, r + 1)
                    A(T1, T1, ACT.Ln, bias=1.0).then_inc(s_msg, 1)
                else:
                    act.wait_ge(s_msg, 3 * r + 2)
                    A(T1, T1, ACT.Exp, scale=-1.0).then_inc(s_msg, 1)

            def head_stage(h, project, attend):
                tiles = [Tile(N_H, h, i) for i in range(5)]
                last = not project
                if attend:
                    v_out, v_copy, level, q_decay, k_decay, kd_copy, square, inverse = hgrn_steps(h - 1)
                    level(0)
                    v_out()
                w_high(tiles[1])
                if attend:
                    level(1)
                    v_copy(0)
                    level(2)
                    v_copy(1)
                    level(3)
                    level(4)
                w_high(tiles[2])
                if project:
                    act.wait_ge(s_mm, 4 * h + 1)
                    A(T1, Z[:, 0, :], ACT.Exp, scale=-1.0).then_inc(s_sg, 1)
                else:
                    gate_step(0, 0)
                if attend:
                    level(5)
                if project:
                    act.wait_ge(s_clamp, 3 * h + 1)
                    A(T1, T1, ACT.Ln, bias=1.0).then_inc(s_sg, 1)
                else:
                    gate_step(0, 1)
                if attend:
                    level(6)
                if project:
                    act.wait_ge(s_sg, 10 * h + 2)
                    A(T1, T1, ACT.Exp, scale=-1.0).then_inc(s_sg, 1)
                else:
                    gate_step(0, 2)
                if attend:
                    q_decay()
                    k_decay()
                w_high(tiles[3])
                if project:
                    act.wait_ge(s_mm, 4 * h + 2)
                    act.wait_ge(s_silu, 2 * h + 1)
                    A(T1, Z[:, 1, :], ACT.Exp, scale=-1.0).then_inc(s_sg, 1)
                if attend:
                    kd_copy(0)
                if project:
                    act.wait_ge(s_clamp, 3 * h + 2)
                    A(T1, T1, ACT.Ln, bias=1.0).then_inc(s_sg, 1)
                    act.wait_ge(s_sg, 10 * h + 5)
                    A(T1, T1, ACT.Exp, scale=-1.0).then_inc(s_sg, 1)
                if attend:
                    kd_copy(1)
                    if last:
                        mem_squares()
                    square(0)
                    if last:
                        mem_inverse()
                        mem_high(0, 0, KB // 2)
                if project:
                    w_high(Tile(N_H, h + 1, 0))
                    act.wait_ge(s_mm, 4 * h + 3)
                    act.wait_ge(s_silu, 2 * h + 2)
                    A(T1, Z[:, 0, :], ACT.Exp, scale=-1.0).then_inc(s_sg, 1)
                    act.wait_ge(s_clamp, 3 * h + 3)
                    A(T2, T1, ACT.Ln, bias=1.0).then_inc(s_sg, 1)
                    act.wait_ge(s_sg, 10 * h + 8)
                    A(T2, T2, ACT.Exp, scale=-1.0).then_inc(s_sg, 1)
                    act.wait_ge(s_k, h + 1)
                    A(T2, T2, ACT.Ln, scale=oml[:, bass.ds(h, 1)], bias=lb[:, bass.ds(h, 1)]).then_inc(s_sg, 1)
                if attend:
                    inverse(0)
                    square(1)
                    if last:
                        mem_high(0, KB // 2, KB)
                    inverse(1)

            act.wait_ge(s_lb, 3)
            act.wait_ge(s_level, 1)
            head_stage(0, True, False)
            with act.Fori(1, HEADS) as h:
                head_stage(h, True, True)
            head_stage(HEADS, False, True)

            def mem_attend(layer, m):
                r = MH * layer + m

                def v_copy():
                    act.wait_ge(s_vmT, r + 1)
                    A(VM[:, :, :], MB[:, 0:2 * P], ACT.Copy).then_inc(s_vm, 1)

                def exps(j):
                    act.wait_ge(s_mneg, 4 * r + j + 1)
                    for a in range(2):
                        e = A(MP[:, j % 2, a, :], SC[:, j % 2, a * MT:(a + 1) * MT], ACT.Exp, scale=MEM_SCALE,
                              bias=sm_neg[:, j % 2, a:a + 1], accum_out=sm_den[:, j % 2, a:a + 1])
                    e.then_inc(s_mexp, 1)

                def p_copy(j):
                    if j == 0 and layer == 0:
                        act.wait_ge(s_mem_out, 16)
                    act.wait_ge(s_mpT, 4 * r + j + 1)
                    A(PTM[:, :, j * 2 * P:(j + 1) * 2 * P], MB[:, :], ACT.Copy).then_inc(s_mpt, 1)

                return v_copy, exps, p_copy

            def mem_stage(base, layer, m, project, attend, gain, last=False):
                r = MH * layer + m
                if attend:
                    v_copy, exps, p_copy = mem_attend(layer, m - 1)
                    act.wait_ge(s_mm, Tile(base, m, 0).n)
                    A(TVM[:, :], Z[:, 1, 0:MT], ACT.Copy).then_inc(s_tvm, 1)
                if project and attend:
                    w_high(Tile(base, m, 1), 20 + 2 * m + 2 if gain else None)
                if attend:
                    v_copy()
                    exps(0)
                    exps(1)
                    p_copy(0)
                    exps(2)
                    p_copy(1)
                    exps(3)
                    p_copy(2)
                    p_copy(3)
                if project and attend:
                    w_high(Tile(base, m, 2))
                    if layer:
                        act.wait_ge(s_mz, m + 1)
                    else:
                        act.wait_ge(s_mm, Tile(base, m, 0).n + 1)
                    sigmoid(Z[:, 0, :], MT1[:, :], s_msg, 3 * r, s_mclamp, r + 1)
                if project:
                    if attend:
                        w_high(Tile(base, m, 3))
                    if layer == 0:
                        act.wait_ge(s_mm, Tile(base, m, 1).n + 1)
                        A(MQ[:, :], Z[:, 1, :], ACT.Copy).then_inc(s_mq, 1)
                    if gain and not last:
                        w_high(Tile(base, m + 1, 0), 20 + 2 * m + 3)
                    else:
                        w_high(Tile(base, m + 1, 0))
                    act.wait_ge(s_mm, Tile(base, m, 2).n + 1)
                    A(KM[:, :], Z[:, 0, 0:MT], ACT.Copy).then_inc(s_km, 1)

            def mem_phase(base, layer):
                gain = layer == 1
                mem_stage(base, layer, 0, True, False, gain)
                with act.Fori(1, MH - gain) as m:
                    mem_stage(base, layer, m, True, True, gain)
                if gain:
                    mem_stage(base, layer, MH - 1, True, True, gain, last=True)

            def out_phase(base, layer):
                v_copy, exps, p_copy = mem_attend(layer, MH - 1)

                def split(*rows):
                    for e in rows:
                        A(X[:, e, :], O[:, e, :], ACT.Copy).then_inc(s_ohi, 1)

                act.wait_ge(s_mm, base)
                A(TVM[:, :], Z[:, 1, 0:MT], ACT.Copy).then_inc(s_tvm, 1)
                if layer == 0:
                    act.wait_ge(s_on, 2 * HEADS)
                else:
                    act.wait_ge(s_so, CH * GROUPS)
                w_high(Tile(base, 0, 0), rows=slice(KB, EB), extra=True)
                v_copy()
                split(0, 1, 2)
                exps(0)
                exps(1)
                split(3)
                p_copy(0)
                split(4)
                exps(2)
                p_copy(1)
                split(5)
                exps(3)
                p_copy(2)
                split(6, 7)
                act.wait_ge(s_mo, 2 * MH * layer + 6)
                split(8, 9, 10)
                p_copy(3)
                w_high(Tile(base, 0, 1), rows=slice(0, EB))
                act.wait_ge(s_mo, 2 * MH * (layer + 1))
                split(11)

                def one(s, i):
                    t = Tile(base, s, i)
                    j = 4 * s + i
                    if 0 < j < KB - 1:
                        w_high(Tile(base, s, i + 1) if i < 3 else Tile(base, s + 1, 0), rows=slice(0, EB))
                    elif j and layer == 0:
                        w_high(Tile(N_K, 0, 0), 1)
                    act.wait_ge(s_mm, t.n + 1)
                    if not (isinstance(s, int) and s == 0 and i < 2):
                        act.wait_ge(s_acc, (KB - 1) * layer + j - 1)
                    A(O[:, 8 + i % 2, :], Z[:, i % 2, :], ACT.Square).then_inc(s_ysq, 1)
                    A(O[:, j, :], Z[:, i % 2, :], ACT.Copy, scale=post_col[:, layer, j:j + 1]).then_inc(s_y, 1)

                act.wait_ge(s_olo, EB * (layer + 1))
                for i in range(4):
                    one(0, i)
                for i in range(4):
                    one(1, i)
                    if layer == 0 and i == 0:
                        act.wait_ge(s_rtg, 1)
                        A(rope_s[:, :], rope_s[:, :], ACT.Sin)
                        A(rope_c[:, :], rope_c[:, :], ACT.Sin).then_inc(s_rope, 1)
                        nc.scalar.preload_act_table_set("natural_log_exp_and_others")
                act.wait_ge(s_yss, layer + 1)
                A(RB[:, :], SCF, ACT.Ln, scale=1.0 / D, bias=eps_c[:, :])\
                    .then_inc(s_rbl, 1)
                act.wait_ge(s_rbl, layer + 1)
                A(RB[:, :], RB[:, :], ACT.Exp, scale=-0.5).then_inc(s_rb, 1)

            mem_phase(N_AM, 0)
            out_phase(N_AO, 0)
            w_high(Tile(N_K, 0, 1), 2)
            for j in range(KB):
                wait_row(act, 0, j)
                A(X[:, j, :], O[:, j, :], ACT.Copy).then_inc(s_xhi, 1)
                if j >= 2:
                    act.wait_ge(s_hss, j - 1)
                A(O[:, 8 + j % 2, :], O[:, j, :], ACT.Square).then_inc(s_hsq, 1)
            act.wait_ge(s_hss, KB)
            A(R2[:, :], SCF, ACT.Ln, scale=1.0 / D, bias=eps_c[:, :]).then_inc(s_rb2l, 1)
            act.wait_ge(s_rb2l, 1)
            A(R2[:, :], R2[:, :], ACT.Exp, scale=-0.5).then_inc(s_rb2, 1)
            w_high(Tile(N_K, 0, 2), 3)
            w_high(Tile(N_K, 0, 3), 4)
            w_high(Tile(N_S, 0, 0), 5)
            for i in range(2):
                for part in range(2):
                    act.wait_ge(s_vsT, 2 * i + part + 1)
                    A(VALL[:, 4 * part:4 * part + 4, i * P:(i + 1) * P], MB[:, :], ACT.Copy).then_inc(s_vs, 1)

            def swa_attend(r):
                def exps(b):
                    lo = P if b == 0 else 0
                    sm = SM[b % 3].rearrange("p (h k) -> p h k", h=4)
                    act.wait_ge(s_sneg, CH * r + b + 1)
                    for h in range(4):
                        A(sm[:, h, lo:], sm[:, h, lo:], ACT.Exp, scale=SWA_SCALE, bias=sm_neg[:, b % 2, h:h + 1],
                          accum_out=sm_den[:, b % 2, h:h + 1])
                    A(sm_snk[:, b % 2, :], sm_snk[:, b % 2, :], ACT.Exp).then_inc(s_sexp, 1)

                def p_copy(b, k):
                    act.wait_ge(s_spT, 15 * r + (2 * b + k if b else 1))
                    if b:
                        act.wait_ge(s_spv, CH * r + b)
                    A(PTS[:, k, :, :], MB[:, :], ACT.Copy).then_inc(s_spt, 1)

                return exps, p_copy

            def swa_stage(g, project, attend):
                tiles = [Tile(N_S, g, i) for i in range(4)]
                if attend:
                    exps, p_copy = swa_attend(g - 1)

                def rounds(i0, i1):
                    for i in range(i0, i1):
                        copies(i)
                        if i < CH:
                            exps(i)

                def copies(i, halves=(0, 1)):
                    for k in halves:
                        if i > 2 or (i == 2 and k == 1):
                            p_copy(i - 2, k)

                def gate(i, step):
                    if step == 0:
                        act.wait_ge(s_zs, 2 * g + i + 1)
                        wait(act, s_sgate, 2 * g + i)
                        A(T1, Z[:, i, :], ACT.Exp, scale=-1.0).then_inc(s_ssg, 1)
                    else:
                        act.wait_ge(s_sclamp, 2 * g + i + 1)
                        A(T1, T1, ACT.Ln, bias=1.0).then_inc(s_ssg, 1)
                        act.wait_ge(s_ssg, 6 * g + 3 * i + 2)
                        A(T1, T1, ACT.Exp, scale=-1.0).then_inc(s_ssg, 1)

                scaled = 4 + 4 * g
                w_high(tiles[1], scaled + 2)
                if attend:
                    rounds(0, 2)
                if project:
                    w_high(tiles[2], scaled + 3)
                    gate(0, 0)
                if attend:
                    rounds(2, 3)
                if project:
                    gate(0, 1)
                if attend:
                    rounds(3, 5)
                if project:
                    w_high(tiles[3], scaled + 4)
                    gate(1, 0)
                else:
                    w_high(tiles[2])
                    gate_step(1, 0)
                if attend:
                    copies(5)
                if project:
                    gate(1, 1)
                else:
                    gate_step(1, 1)
                    gate_step(1, 2)
                if attend:
                    exps(5)
                    rounds(6, 7)
                    copies(7)
                if project:
                    w_high(Tile(N_S, g + 1, 0), scaled + 5)
                if attend:
                    exps(7)
                    if not project:
                        w_high(tiles[3])
                    rounds(CH, CH + 1)
                    if not project:
                        mem_high(1, 0, KB)
                    rounds(CH + 1, CH + 2)
                if project:
                    if isinstance(g, int) and g == 0:
                        act.wait_ge(s_vs, 4)
                    else:
                        act.wait_ge(s_spv, CH * g)
                    A(VG[:, :, :], VALL[:, :, bass.ds(g * DH, DH)], ACT.Copy).then_inc(s_vg, 1)

            swa_stage(0, True, False)
            with act.Fori(1, GROUPS) as g:
                swa_stage(g, True, True)
            swa_stage(GROUPS, False, True)
            mem_phase(N_BM, 1)
            out_phase(N_BO, 1)
        @block.vector
        def _(dve):
            TT = nc.vector.tensor_tensor
            STT = nc.vector.scalar_tensor_tensor
            TS = nc.vector.tensor_scalar

            def w_low(t, rows=slice(0, KB), extra=False):
                dve.wait_ge(s_whi_x if extra else s_whi, (1 + (t.n > N_AO)) if extra else t.n + 1)
                TT(w_lo[:, t.slot, rows, :], w_raw[:, t.slot, rows, :], w_hi[:, t.slot, rows, :].bitcast(F32),
                   ALU.subtract).then_inc(s_wlo_x if extra else s_wlo, 1)

            nc.vector.memset(ones[:, :], 1.0).then_inc(s_memset, 1)
            nc.vector.memset(eps_c[:, :], EPS).then_inc(s_memset, 1)
            for i in range(KB // 2):
                dve.wait_ge(s_xsq, 2 * i + 2)
                if i >= 2:
                    dve.wait_ge(s_xss, i - 1)
                TT(E2[:, i % 2, :], KH[:, 0, :], KH[:, 1, :], ALU.add).then_inc(s_xadd, 1)
            dve.wait_ge(s_const, 16 * N_CONST)
            w_low(Tile(N_H, 0, 0))
            dve.wait_ge(s_rb0, 1)

            def x_low(e):
                dve.wait_ge(s_xhi, e + 1)
                STT(X[:, 8 + e, :], O[:, e, :], pre_col[:, 0, e:e + 1], X[:, e, :].bitcast(F32), ALU.mult,
                    ALU.subtract).then_inc(s_xlo, 1)

            for e in range(0, KB, 2):
                TT(O[:, e, :], O[:, e, :], RB0[:, :], ALU.mult).then_inc(s_xs, 1)
                if e >= 2:
                    x_low(e - 2)
                    x_low(e - 1)
            x_low(KB - 2)
            x_low(KB - 1)
            dve.wait_ge(s_level_in, 16)
            nc.vector.tensor_copy(level_mask[:, :, :], LMF).then_inc(s_level, 1)
            TT(lb[:, :], lb2[:, 0, :], lb2[:, 1, :], ALU.max).then_inc(s_memset, 1)
            dve.wait_ge(s_memset, 3)
            TT(lb2[:, :, :], lb2[:, :, :], bc(lb[:, :], 2), ALU.subtract).then_inc(s_lbd, 1)
            dve.wait_ge(s_lb, 1)
            TT(lb[:, :], lbt[:, 0, :], lbt[:, 1, :], ALU.add).then_inc(s_lbd, 1)
            dve.wait_ge(s_lbd, 2)
            nc.vector.reciprocal(lb[:, :], lb[:, :]).then_inc(s_lbd, 1)
            dve.wait_ge(s_lbd, 3)
            TT(oml[:, :], lb[:, :], lbt[:, 1, :], ALU.mult).then_inc(s_lb, 1)
            TT(lb[:, :], lb[:, :], lbt[:, 0, :], ALU.mult).then_inc(s_lb, 1)

            def clamp(tmp, steps, at, sem_):
                dve.wait_ge(steps, at)
                TS(tmp, tmp, BIG, None, ALU.min).then_inc(sem_, 1)

            def hgrn_steps(r):
                def dif(l):
                    half = 1 << l
                    e = E2[:, l % 2, :].rearrange("p (n b) -> p n b", b=2 * half)
                    c = CUM[:, :].rearrange("p (n b) -> p n b", b=2 * half)
                    if l == 0:
                        dve.wait_ge(s_cum, r + 1)
                    if l >= 2:
                        dve.wait_ge(s_hat, LEVELS * r + l - 1)
                    TT(e, c, c[:, :, half - 1:half].to_broadcast([P, T // (2 * half), 2 * half]), ALU.subtract)\
                        .then_inc(s_dif, 1)

                def dif_end():
                    dve.wait_ge(s_hat, LEVELS * r + LEVELS)
                    c = CUM[:, :].rearrange("p (n b) -> p n b", b=P)
                    TT(E2[:, 0, :].rearrange("p (n b) -> p n b", b=P), c[:, :, P - 1:P].to_broadcast([P, CH, P]), c,
                       ALU.subtract).then_inc(s_dif, 1)

                def diagonal(part):
                    dve.wait_ge(s_diag, 2 * r + part + 1)
                    TT(PT[:, part * HALF:(part + 1) * HALF].rearrange("p (c t) -> p c t", c=4),
                       SC[:, part, :].rearrange("p (c t) -> p c t", c=4), bc(ident[:, :], 4), ALU.mult)\
                        .then_inc(s_diag_ev, 1)

                def merge(l):
                    half = 1 << l
                    if l == 0:
                        dve.wait_ge(s_diag_ev, 2 * r + 2)
                    else:
                        dve.wait_ge(s_pred, LEVELS * r + l)
                    dve.wait_ge(s_lev, LEVELS * r + l + 1)
                    nc.vector.memset(pad[:, :], 0.0)
                    nc.vector.copy_predicated(
                        PT[:, :].rearrange("p (n f i) -> p n f i", f=2, i=half)[:, :, 1, :],
                        level_mask[:, l, :].rearrange("p (n i) -> p n i", i=half),
                        SC[:, l % 2, :].rearrange("p (n i) -> p n i", i=half)).then_inc(s_pred, 1)

                def state(c):
                    dve.wait_ge(s_stm, (CH - 1) * r + c + 1)
                    st = MB[:, 0:P]
                    if c == 0:
                        i = nc.vector.tensor_copy(ST[:, 1, :], st)
                    else:
                        dve.wait_ge(s_el, r + 1)
                        dve.wait_ge(s_st, (CH - 1) * r + c)
                        i = STT(ST[:, (c + 1) % 2, :], ST[:, c % 2, :], EL[:, c:c + 1], st, ALU.mult, ALU.add)
                    i.then_inc(s_st, 1)

                def gate(part):
                    o = O[:, bass.ds(r, 1), part * HALF:(part + 1) * HALF]
                    dve.wait_ge(s_osq, 2 * r + part + 1)
                    STT(o, OB[:, :].unsqueeze(1), out_col[:, bass.ds(r, 1)], o, ALU.mult, ALU.mult).then_inc(s_og, 1)

                return dif, dif_end, diagonal, merge, state, gate

            def mem_low(layer, first, end):
                for e in range(first, end):
                    dve.wait_ge(s_mhi, KB * layer + e + 1)
                    i = STT(MLO[:, e, :], MS[layer][:, e, :], mem_col[:, layer, e:e + 1], MHI[:, e, :].bitcast(F32),
                            ALU.mult, ALU.subtract)
                    if e % 2:
                        i.then_inc(s_mlo, 1)

            def mem_gate(layer):
                r = MH * layer
                dve.wait_ge(s_msg, 3 * r + 3)
                TT(O[:, 8, :], Z[:, 0, :], T1, ALU.mult).then_inc(s_mgate, 1)

            def head_stage(h, project, attend):
                if attend:
                    dif, dif_end, diagonal, merge, state, gate = hgrn_steps(h - 1)
                w_low(Tile(N_H, h, 1))
                if attend:
                    diagonal(0)
                    diagonal(1)
                    dif(2)
                    merge(0)
                    dif(3)
                    dif(4)
                    merge(1)
                w_low(Tile(N_H, h, 2))
                if project:
                    clamp(T1, s_sg, 10 * h + 1, s_clamp)
                else:
                    clamp(T1, s_msg, 1, s_mclamp)
                if attend:
                    dif(5)
                    merge(2)
                    dif(6)
                    merge(3)
                    merge(4)
                if project:
                    dve.wait_ge(s_sg, 10 * h + 3)
                    TT(Q[:, bass.ds(h % 2, 1), :], Z[:, 0:1, :], T1.unsqueeze(1), ALU.mult).then_inc(s_silu, 1)
                else:
                    mem_gate(0)
                if attend:
                    dif_end()
                    merge(5)
                w_low(Tile(N_H, h, 3))
                if project:
                    clamp(T1, s_sg, 10 * h + 4, s_clamp)
                if attend:
                    merge(6)
                if project:
                    dve.wait_ge(s_sg, 10 * h + 6)
                    TT(O[:, bass.ds(h, 1), :], Z[:, 1:2, :], T1.unsqueeze(1), ALU.mult).then_inc(s_silu, 1)
                if attend:
                    for c in range(4):
                        state(c)
                    gate(0)
                if project:
                    w_low(Tile(N_H, h + 1, 0))
                if attend:
                    state(4)
                if project:
                    clamp(T1, s_sg, 10 * h + 7, s_clamp)
                if attend:
                    state(5)
                if project:
                    dve.wait_ge(s_sg, 10 * h + 9)
                    dve.wait_ge(s_clamp, 3 * h + 3)
                    STT(KK[:, :], T1, oml[:, bass.ds(h, 1)], T2, ALU.mult, ALU.mult).then_inc(s_k, 1)
                if attend:
                    state(6)
                if project:
                    dve.wait_ge(s_sg, 10 * h + 10)
                    for c in range(CH):
                        i = nc.vector.tensor_tensor_scan(CUM[:, c * P:(c + 1) * P], ones[:, :], T2[:, c * P:(c + 1) * P],
                                                         0.0, ALU.mult, ALU.add)
                    i.then_inc(s_cum, 1)
                    next_dif = hgrn_steps(h)[0]
                    next_dif(0)
                    next_dif(1)
                else:
                    mem_low(0, 0, KB // 2)
                if attend:
                    gate(1)
                if not project:
                    mem_low(0, KB // 2, KB)

            head_stage(0, True, False)
            with dve.Fori(1, HEADS) as h:
                head_stage(h, True, True)
            head_stage(HEADS, False, True)

            def mem_attend(layer, m):
                r = MH * layer + m

                def maximum(j):
                    dve.wait_ge(s_msc, 4 * r + j + 1)
                    nc.vector.tensor_reduce(sm_max[:, j % 2, 0:2], SC[:, j % 2, :].rearrange("p (a m) -> p a m", a=2),
                                            AX.X, ALU.max).then_inc(s_mmax, 1)
                    dve.wait_ge(s_mmax, 4 * r + j + 1)
                    TS(sm_neg[:, j % 2, 0:2], sm_max[:, j % 2, 0:2], -MEM_SCALE, None, ALU.mult).then_inc(s_mneg, 1)

                def normalise(j):
                    dve.wait_ge(s_mexp, 4 * r + j + 1)
                    nc.vector.reciprocal(sm_inv[:, j % 2, 0:2], sm_den[:, j % 2, 0:2]).then_inc(s_minv, 1)
                    dve.wait_ge(s_minv, 4 * r + j + 1)
                    for a in range(2):
                        i = TS(MP[:, j % 2, a, :], MP[:, j % 2, a, :], sm_inv[:, j % 2, a:a + 1], None, ALU.mult)
                    i.then_inc(s_mpn, 1)

                def gate(half):
                    dve.wait_ge(s_mpv, 2 * r + half + 1)
                    o = O[:, bass.ds(m + 8, 1), half * HALF:(half + 1) * HALF]
                    TT(o, OB[:, :].unsqueeze(1), o, ALU.mult).then_inc(s_mo, 1)

                return maximum, normalise, gate

            def mem_stage(base, layer, m, project, attend):
                r = MH * layer + m
                if attend:
                    maximum, normalise, gate = mem_attend(layer, m - 1)
                    maximum(0)
                if project and attend:
                    w_low(Tile(base, m, 1))
                if attend:
                    maximum(1)
                    normalise(0)
                    maximum(2)
                    normalise(1)
                    maximum(3)
                    normalise(2)
                    normalise(3)
                if project and attend:
                    w_low(Tile(base, m, 2))
                    if layer:
                        dve.wait_ge(s_mm, Tile(base, m, 0).n + 1)
                        TT(Z[:, 0, :], Z[:, 0, :], R2[:, :], ALU.mult).then_inc(s_mz, 1)
                    clamp(MT1[:, :], s_msg, 3 * r + 1, s_mclamp)
                    gate(0)
                    dve.wait_ge(s_msg, 3 * r + 3)
                    TT(O[:, bass.ds(m + 8, 1), :], Z[:, 0:1, :], MT1[:, :].unsqueeze(1), ALU.mult).then_inc(s_mgate, 1)
                if attend:
                    gate(1)
                if project:
                    if layer:
                        dve.wait_ge(s_mm, Tile(base, m, 1).n + 1)
                        TT(MQ[:, :], Z[:, 1, :], R2[:, :], ALU.mult).then_inc(s_mq, 1)
                    if attend:
                        w_low(Tile(base, m, 3))
                    w_low(Tile(base, m + 1, 0))

            def link(i, at):
                i.then_inc(s_rt, 1)
                dve.wait_ge(s_rt, at)

            def rope_angle():
                ang, k = rope_c[:, :], rope_s[:, :]
                dve.wait_ge(s_pos, 16)
                link(nc.vector.tensor_copy(ang, RTI[:, :]), 1)
                link(TS(ang, ang, freq[:, 0:1], None, ALU.mult), 2)
                link(TS(k, ang, 1.0 / (2 * PI), None, ALU.mult), 3)
                link(nc.vector.tensor_copy(RTI[:, :], k), 4)
                link(nc.vector.tensor_copy(k, RTI[:, :]), 5)

            def rope_reduce():
                ang, k = rope_c[:, :], rope_s[:, :]
                c1 = 6.28125
                c2 = float(np.float32(np.round((2 * np.pi - c1) * 2 ** 22) / 2 ** 22))
                c3 = float(2 * np.pi - c1 - c2)
                for i, c in enumerate((c1, c2, c3)):
                    link(STT(ang, k, -c, ang, ALU.mult, ALU.add), 6 + i)

            def rope_wrap():
                ang, k = rope_c[:, :], RTK[:, :]
                link(TS(k, ang, PI, -2 * PI, ALU.is_gt, ALU.mult), 9)
                link(TT(ang, ang, k, ALU.add), 10)
                link(TS(k, ang, -PI, 2 * PI, ALU.is_lt, ALU.mult), 11)
                link(TT(ang, ang, k, ALU.add), 12)

            def rope_cosine():
                ang, k = rope_c[:, :], RTK[:, :]
                top = 3.1415925
                link(TS(rope_s[:, :], ang, top, -top, ALU.min, ALU.max), 13)
                link(TS(ang, ang, PI / 2, None, ALU.add), 14)
                link(TS(k, ang, PI, -2 * PI, ALU.is_gt, ALU.mult), 15)
                link(TT(ang, ang, k, ALU.add), 16)
                TS(ang, ang, top, -top, ALU.min, ALU.max).then_inc(s_rtg, 1)

            def mem_phase(base, layer):
                mem_stage(base, layer, 0, True, False)
                with dve.Fori(1, MH) as m:
                    mem_stage(base, layer, m, True, True)

            def out_phase(base, layer):
                maximum, normalise, gate = mem_attend(layer, MH - 1)

                def split(*rows):
                    for e in rows:
                        dve.wait_ge(s_ohi, EB * layer + e + 1)
                        TT(low_row(e), O[:, e, :], X[:, e, :].bitcast(F32), ALU.subtract).then_inc(s_olo, 1)

                w_low(Tile(base, 0, 0), rows=slice(KB, EB), extra=True)
                split(0, 1)
                maximum(0)
                maximum(1)
                split(2)
                normalise(0)
                split(3)
                maximum(2)
                normalise(1)
                split(4)
                maximum(3)
                normalise(2)
                split(5)
                normalise(3)
                split(6)
                gate(0)
                split(7, 8)
                dve.wait_ge(s_mpT, 4 * MH * (layer + 1))
                split(9)
                gate(1)
                split(10, 11)
                for j in range(1, KB):
                    w_low(Tile(base, j // 4, j % 4), rows=slice(0, EB))
                    if layer == 0 and j < 5:
                        (rope_angle, rope_reduce, rope_wrap, rope_cosine)[j - 1]()
                if layer == 0:
                    w_low(Tile(N_K, 0, 0))
                dve.wait_ge(s_rb, layer + 1)
                low = 0
                for i, j in enumerate(DVE_ROWS[layer]):
                    dve.wait_ge(s_hr[j], 16 * (layer + 1))
                    TT(O[:, j, :], O[:, j, :], RB[:, :], ALU.mult).then_inc(s_yn, 1)
                    dve.wait_ge(s_yn, layer * len(DVE_ROWS[0]) + i + 1)
                    TT(O[:, j, :], O[:, j, :], HR[:, j, :], ALU.add).then_inc(s_h, 1)
                    if layer == 0:
                        until = max(0, j - 1) if i + 1 < len(DVE_ROWS[0]) else KB
                        for e in range(low, until):
                            dve.wait_ge(s_xhi, KB + e + 1)
                            TT(X[:, 8 + e, :], O[:, e, :], X[:, e, :].bitcast(F32), ALU.subtract).then_inc(s_xlo, 1)
                        low = until

            mem_phase(N_AM, 0)
            out_phase(N_AO, 0)
            w_low(Tile(N_K, 0, 1))
            dve.wait_ge(s_rope, 1)
            dve.wait_ge(s_rb2, 1)
            TT(rope_c[:, :], rope_c[:, :], R2[:, :], ALU.mult).then_inc(s_rt, 1)
            TT(rope_s[:, :], rope_s[:, :], R2[:, :], ALU.mult).then_inc(s_rt, 1)
            dve.wait_ge(s_rt, 18)

            def rotate(slot, before, to, ra):
                z = Z[:, slot, :]
                wait(dve, s_rot, before)
                TT(ra, z, rope_c[:, :], ALU.mult).then_inc(s_ra, 1)
                TT(z, z, rope_s[:, :], ALU.mult).then_inc(s_ra, 1)
                dve.wait_ge(s_ra, 2 * (before + 1))
                TT(to[0:64, :], ra[0:64, :], Z[64:128, slot, :], ALU.subtract)
                TT(to[64:128, :], ra[64:128, :], Z[0:64, slot, :], ALU.add).then_inc(s_rot, 1)

            for i in range(2):
                w_low(Tile(N_K, 0, i + 2))
                dve.wait_ge(s_mm, N_K + i + 1)
                rotate(i, i, KST[:, i, :], RA)
            for i, to in enumerate((T1, RA)):
                dve.wait_ge(s_mm, N_K + 3 + i)
                if i:
                    dve.wait_ge(s_rot, 2)
                TT(to, Z[:, i, :], R2[:, :], ALU.mult).then_inc(s_tvs, 1)
                if i == 0:
                    w_low(Tile(N_S, 0, 0))
            for stored in s_h_out:
                dve.wait_ge(stored, 16 * KB // 2)

            def swa_attend(r):
                def mask(b):
                    lo = P if b == 0 else 0
                    sm = SM[b % 3].rearrange("p (h k) -> p h k", h=4)
                    if b >= 3:
                        dve.wait_ge(s_spT, 15 * r + 2 * (b - 3) + 1)
                    for p in range(2):
                        dve.wait_ge(s_sc, 16 * r + 2 * b + p + 1)
                        TT(sm[:, 2 * p:2 * p + 2, lo:], SC[:, p, :].rearrange("p (h k) -> p h k", h=2)[:, :, lo:],
                           bc(window[:, lo:], 2), ALU.add).then_inc(s_msk, 1)
                    dve.wait_ge(s_msk, 16 * r + 2 * b + 2)
                    nc.vector.tensor_reduce(sm_max[:, b % 2, :], sm[:, :, lo:], AX.X, ALU.max).then_inc(s_smax, 1)
                    dve.wait_ge(s_smax, CH * r + b + 1)
                    sink = sink_b[:, bass.ds(4 * r, 4)]
                    STT(sm_max[:, b % 2, :], sm_max[:, b % 2, :], SWA_SCALE, sink, ALU.mult, ALU.max).then_inc(s_sm, 1)
                    dve.wait_ge(s_sm, 2 * (CH * r + b) + 1)
                    TT(sm_snk[:, b % 2, :], sink, sm_max[:, b % 2, :], ALU.subtract).then_inc(s_sm, 1)
                    TS(sm_neg[:, b % 2, :], sm_max[:, b % 2, :], -1.0, None, ALU.mult).then_inc(s_sneg, 1)

                def normalise(b):
                    lo = P if b == 0 else 0
                    sm = SM[b % 3].rearrange("p (h k) -> p h k", h=4)
                    dve.wait_ge(s_sexp, CH * r + b + 1)
                    TT(sm_den[:, b % 2, :], sm_den[:, b % 2, :], sm_snk[:, b % 2, :], ALU.add).then_inc(s_sden, 1)
                    dve.wait_ge(s_sden, CH * r + b + 1)
                    nc.vector.reciprocal(sm_inv[:, b % 2, :], sm_den[:, b % 2, :]).then_inc(s_sinv, 1)
                    dve.wait_ge(s_sinv, CH * r + b + 1)
                    for h in range(4):
                        i = TS(sm[:, h, lo:], sm[:, h, lo:], sm_inv[:, b % 2, h:h + 1], None, ALU.mult)
                    i.then_inc(s_spn, 1)

                def gate(b):
                    dve.wait_ge(s_spv, CH * r + b + 1)
                    o = O[:, bass.ds(2 * r, 2), b * P:(b + 1) * P]
                    TT(o, OB[:, 0:2 * P].rearrange("p (a t) -> p a t", a=2), o,
                       ALU.mult).then_inc(s_so, 1)

                return mask, normalise, gate

            def swa_stage(g, project, attend):
                if attend:
                    mask, normalise, gate = swa_attend(g - 1)

                def round_(i):
                    if attend and i < CH:
                        mask(i)
                    if attend and 1 <= i <= CH:
                        normalise(i - 1)
                    if attend and i >= 2:
                        gate(i - 2)

                def scale(i):
                    dve.wait_ge(s_mm, Tile(N_S, g, i).n + 1)
                    TT(Z[:, i, :], Z[:, i, :], R2[:, :], ALU.mult).then_inc(s_zs if project else s_mz, 1)

                def silu(i):
                    dve.wait_ge(s_ssg, 6 * g + 3 * i + 3)
                    TT(O[:, bass.ds(2 * g + i, 1), :], Z[:, i:i + 1, :], T1.unsqueeze(1), ALU.mult).then_inc(s_sgate, 1)

                if attend:
                    dve.wait_ge(s_mm, Tile(N_S, g, 0).n)
                    rotate(1, 2 + 2 * (g - 1) + 1, QR[:, 1, :], RA)
                w_low(Tile(N_S, g, 1))
                round_(0)
                round_(1)
                if project:
                    w_low(Tile(N_S, g, 2))
                    scale(0)
                round_(2)
                if project:
                    clamp(T1, s_ssg, 6 * g + 1, s_sclamp)
                round_(3)
                if project:
                    silu(0)
                round_(4)
                w_low(Tile(N_S, g, 3 if project else 2))
                scale(1 if project else 0)
                if project:
                    clamp(T1, s_ssg, 6 * g + 4, s_sclamp)
                else:
                    clamp(T1, s_msg, 3 * MH + 1, s_mclamp)
                round_(5)
                if project:
                    silu(1)
                else:
                    mem_gate(1)
                round_(6)
                round_(7)
                w_low(Tile(N_S, g + 1, 0) if project else Tile(N_S, g, 3))
                round_(CH)
                if project:
                    dve.wait_ge(s_mm, Tile(N_S, g, 2).n + 1)
                    rotate(0, 2 + 2 * g, QR[:, 0, :], RA)
                else:
                    mem_low(1, 0, KB)
                round_(CH + 1)

            swa_stage(0, True, False)
            with dve.Fori(1, GROUPS) as g:
                swa_stage(g, True, True)
            swa_stage(GROUPS, False, True)
            mem_phase(N_BM, 1)
            out_phase(N_BO, 1)

        @block.gpsimd
        def _(pool):
            GT = nc.gpsimd.tensor_tensor
            pool.wait_ge(s_xss, KB // 2)
            nc.gpsimd.memset(KH[:, :, :], 0.0).then_inc(s_kz, 1)
            pool.wait_ge(s_rb0, 1)
            for e in range(1, KB, 2):
                GT(O[:, e, :], O[:, e, :], RB0[:, :], ALU.mult).then_inc(s_xp, 1)
            pool.wait_ge(s_kz, 1)

            def mem_multiply():
                pool.wait_ge(s_rbm, 2)
                for e in range(0, KB, 2):
                    m = MS[0][:, e:e + 2, :]
                    GT(m, m, bc(RBM, 2), ALU.mult).then_inc(s_mx, 1)

            def hgrn(r, last=False):
                q1 = Q[:, bass.ds(r % 2, 1), :].rearrange("p a t -> p (a t)")
                pool.wait_ge(s_silu, 2 * r + 1)
                for l in range(LEVELS):
                    half = 1 << l

                    def halves(ap):
                        return ap.rearrange("p (n f i) -> p n f i", f=2, i=half)

                    e = halves(E2[:, l % 2, :])
                    pool.wait_ge(s_dec, 9 * r + l + 1)
                    if l >= 2:
                        pool.wait_ge(s_lev, LEVELS * r + l - 1)
                    GT(halves(KH[:, l % 2, :])[:, :, 0, :], halves(KK[:, :])[:, :, 0, :], e[:, :, 0, :], ALU.mult)
                    GT(QH[:, l % 2, :].rearrange("p (n i) -> p n i", i=half), halves(q1)[:, :, 1, :], e[:, :, 1, :],
                       ALU.mult).then_inc(s_hat, 1)
                pool.wait_ge(s_dec, 9 * r + 8)
                pool.wait_ge(s_diag, 2 * r + 2)
                pool.wait_ge(s_hat, LEVELS * (r + 1))
                GT(q1, q1, E2[:, 1, :], ALU.mult).then_inc(s_qc, 1)
                pool.wait_ge(s_dec, 9 * r + 9)
                GT(E2[:, 0, :], KK[:, :], E2[:, 0, :], ALU.mult).then_inc(s_kd, 1)
                if last:
                    mem_multiply()
                for part in range(2):
                    o = O[:, bass.ds(r, 1), part * HALF:(part + 1) * HALF]
                    pool.wait_ge(s_rn, 2 * r + part + 1)
                    pool.wait_ge(s_og, 2 * r + part + 1)
                    GT(o, o, RN[:, :].unsqueeze(1), ALU.mult).then_inc(s_on, 1)

            hgrn(0)
            with pool.Fori(1, HEADS - 1) as r:
                hgrn(r)
            hgrn(HEADS - 1, last=True)

            def out_phase(layer):
                acc = O[:, 10, :]
                for j in range(KB - 1):
                    pool.wait_ge(s_ysq, KB * layer + j + 1)
                    if j == 0:
                        nc.gpsimd.tensor_copy(acc, O[:, 8, :]).then_inc(s_acc, 1)
                    else:
                        pool.wait_ge(s_acc, (KB - 1) * layer + j)
                        GT(acc, acc, O[:, 8 + j % 2, :], ALU.add).then_inc(s_acc, 1)
                if layer == 0:
                    scale(Tile(N_K, 0, 0), kv_col[:, :])
                    scale(Tile(N_K, 0, 1), kv_col[:, :])
                pool.wait_ge(s_rb, layer + 1)
                for i, j in enumerate(POOL_ROWS[layer]):
                    pool.wait_ge(s_hr[j], 16 * (layer + 1))
                    GT(O[:, j, :], O[:, j, :], RB[:, :], ALU.mult).then_inc(s_yp, 1)
                    pool.wait_ge(s_yp, layer * len(POOL_ROWS[0]) + i + 1)
                    GT(O[:, j, :], O[:, j, :], HR[:, j, :], ALU.add).then_inc(s_hp, 1)

            def scale(t, col):
                pool.wait_ge(s_w_in[t.slot], 16 * (t.before + 1))
                w = w_raw[:, t.slot, 0:KB, :]
                GT(w, w, col.unsqueeze(2).to_broadcast([P, KB, P]), ALU.mult).then_inc(s_w_scaled, 1)

            pool.wait_ge(s_mpv, 2 * MH)
            pool.dma_start(RTI[:, :], positions.to_broadcast([P, T])).then_inc(s_pos, 16)
            out_phase(0)
            for i in range(2, 4):
                scale(Tile(N_K, 0, i), kv_col[:, :])
            scale(Tile(N_S, 0, 0), pre_col[:, 1, :])
            for i in range(2):
                pool.wait_ge(s_rot, i + 1)
                for f in range(2):
                    for hh in range(2):
                        pool.dma_start(k_dram[2 * i + hh, f], KST[64 * f + 32 * hh:64 * f + 32 * hh + 32, i, :])\
                            .then_inc(s_k_out, 16)
            nc.gpsimd.memset(KP[:, :, :], 0.0).then_inc(s_kz, 1)
            pool.wait_ge(s_kz, 2)
            pool.wait_ge(s_k_out, 16 * 8)

            def swa(g, first=False):
                for i in range(1, 4):
                    scale(Tile(N_S, g, i), pre_col[:, 1, :])
                scale(Tile(N_S, g + 1, 0), pre_col[:, 1, :])
                if not first:
                    pool.wait_ge(s_sc, 16 * g)
                for odd in range(2):
                    for f in range(2):
                        at = 64 * f + 32 * odd
                        pool.dma_start(KP[at:at + 32, odd, :], k_dram[bass.ds(g, 1), f].rearrange("a i t -> (a i) t"))\
                            .then_inc(s_kp, 16)

            swa(0, True)
            with pool.Fori(1, GROUPS) as g:
                swa(g)

            def mem_scale(m):
                scale(Tile(N_BM, m, 1), pre_col[:, 1, :])
                scale(Tile(N_BM, m + 1, 0), pre_col[:, 1, :])

            mem_scale(0)
            with pool.Fori(1, MH - 1) as m:
                mem_scale(m)
            scale(Tile(N_BM, MH - 1, 1), pre_col[:, 1, :])
            out_phase(1)


def constants():
    ident = np.eye(P, dtype=np.float32)
    s = np.arange(P)[:, None]
    level = np.zeros((P, LEVELS, CH, P // 2), np.float32)
    for l in range(LEVELS):
        half = 1 << l
        t = np.arange(P).reshape(-1, 2, half)[:, 1, :].reshape(1, -1)
        level[:, l] = ((s // (2 * half) == t // (2 * half)) & (s // half % 2 == 0))[:, None, :]
    q = np.arange(P)[:, None]
    k = np.arange(2 * P)[None, :]
    window = np.where((k > q) & (k <= q + P), 0.0, NEG).astype(np.float32)
    i = np.arange(P) % (DH // 2)
    freq = (10000.0 ** (-2.0 * i / DH)).astype(np.float32).reshape(P, 1)
    return {"c_ident": ident, "c_level": level.reshape(P, LEVELS, HALF), "c_window": window, "c_freq": freq}


def _tiles(w):
    return w.reshape(-1, P, w.shape[1] // P, P).transpose(2, 1, 0, 3)


def _columns(v):
    v = v.reshape(v.shape[:-1] + (-1, P))
    return np.moveaxis(v, -1, 0)


def _rotary(w):
    return w.reshape(w.shape[0], -1, 2, 2, DH // 2).transpose(0, 1, 3, 2, 4).reshape(w.shape)


def _features(a):
    return a.T.reshape(-1, P, a.shape[0]).transpose(1, 0, 2)


def _layout(i):
    b = i["b_w_in"][0]
    kv = i["w_kv_shared"]
    return [
        ("x", _features(i["x"][0])), ("mem", _features(i["mem"][0])), ("positions", i["positions"]),
        ("pre", _columns(i["pre_norm_g"])), ("post", _columns(i["post_norm_g"])), ("memg", _columns(i["mem_norm_g"])),
        ("wmem", np.concatenate([_tiles(w) for w in i["w_mem_kv"]])), ("awin", _tiles(i["a_w_in"][0])),
        ("lb", _columns(i["a_lb_logits"])), ("outg", _columns(i["a_out_norm_g"][0])), ("awout", _tiles(i["a_w_out"][0])),
        ("kvg", _columns(i["kv_norm_g"])),
        ("wkv", _tiles(np.concatenate([_rotary(kv[:, :GROUPS * DH]), kv[:, GROUPS * DH:]], 1))),
        ("bwin", _tiles(np.concatenate([_rotary(b[:, :D]), b[:, D:]], 1))),
        ("sinks", i["b_sinks"]), ("bwout", _tiles(i["b_w_out"][0])),
    ]


def kernel(**inputs):
    import concourse.bacc as bacc
    from concourse.bass_utils import run_bass_kernel_spmd as run

    nc = bacc.Bacc("TRN2", target_bir_lowering=False, num_devices=1)
    arrays, args = {}, []
    for name, a in _layout({n: np.asarray(a) for n, a in inputs.items()}) + list(constants().items()):
        a = np.ascontiguousarray(a)
        arrays[f"in_{name}"] = a
        args.append(nc.dram_tensor(f"in_{name}", a.shape, mybir.dt.from_np(a.dtype), kind="ExternalInput").ap())
    args.append(nc.dram_tensor("h_scratch", (P, KB, T), F32, kind="Internal").ap())
    args.append(nc.dram_tensor("k_scratch", (GROUPS, 2, DH // 2, T), F32, kind="Internal").ap())
    args.append(nc.dram_tensor("m_scratch", (P, KB, MT), F32, kind="Internal").ap())
    args.append(nc.dram_tensor("out_0", (P, KB, T), F32, kind="ExternalOutput").ap())
    build(nc, *args)
    r = run(nc, [arrays], core_ids=[0])
    return np.ascontiguousarray(r.results[0]["out_0"].transpose(2, 1, 0).reshape(1, T, D))
```
